# Optimizing a Trainium2 kernel written in Bass

```python
import math
import jax, jax.numpy as jnp
from jax import lax
import numpy as np

D_MODEL = 1024
BATCH = 1
SEQ = 512
DEPTH = 2

N_MIXERS = 3
N_HEADS = 8
HEAD_DIM = 128
WIDTH = N_HEADS * HEAD_DIM
ROPE_THETA = 10000.0
NORM_EPS = 1e-6
Q_BLOCK = 128
MOBA_BLOCK = 256
MOBA_TOPK = 3
MOBA_Q_CHUNK = 8
DIFF_SUB_DIM = HEAD_DIM // 2
DIFF_LAMBDA_STD = 0.1

kernel_name = "hybrid_moba_fox_diffattn_gated"

def _layers_of(kind):
    return len(range(kind, DEPTH, N_MIXERS))

def rms_norm(x, g):
    x32 = x.astype(jnp.float32)
    y = x32 * lax.rsqrt(jnp.mean(x32 * x32, axis=-1, keepdims=True) + NORM_EPS)
    return (y * g.astype(jnp.float32)).astype(x.dtype)

def rope_tables(seq, dim):
    inv = 1.0 / (ROPE_THETA ** (jnp.arange(0, dim, 2, dtype=jnp.float32) / dim))
    ang = jnp.arange(seq, dtype=jnp.float32)[:, None] * inv[None, :]
    return jnp.cos(ang), jnp.sin(ang)

def apply_rope(x, cos, sin):
    x32 = x.astype(jnp.float32)
    x1, x2 = jnp.split(x32, 2, axis=-1)
    out = jnp.concatenate([x1 * cos - x2 * sin, x2 * cos + x1 * sin], axis=-1)
    return out.astype(x.dtype)

def split_heads(t, n):
    b, s, _ = t.shape
    return t.reshape(b, s, n, -1).transpose(0, 2, 1, 3)

def merge_heads(t):
    b, h, s, d = t.shape
    return t.transpose(0, 2, 1, 3).reshape(b, s, h * d)

def gather_blocks(blocks, idx):
    return jax.vmap(jax.vmap(lambda bl, ix: bl[ix]))(blocks, idx)

def moba_attention(q, k, v):
    b, h, s, d = q.shape
    nb = -(-s // MOBA_BLOCK)
    pad = nb * MOBA_BLOCK - s
    kb = jnp.pad(k, ((0, 0), (0, 0), (0, pad), (0, 0))).reshape(b, h, nb, MOBA_BLOCK, d)
    vb = jnp.pad(v, ((0, 0), (0, 0), (0, pad), (0, 0))).reshape(b, h, nb, MOBA_BLOCK, d)
    topk = min(MOBA_TOPK, nb - 1)
    scale = d ** -0.5
    if topk > 0:
        k_mean = jnp.mean(kb.astype(jnp.float32), axis=3)
        gate = jnp.einsum('bhsd,bhnd->bhsn', q, k_mean.astype(q.dtype),
                          preferred_element_type=jnp.float32)
        q_blk = jnp.arange(s) // MOBA_BLOCK
        past = jnp.arange(nb)[None, :] < q_blk[:, None]
        gate = jnp.where(past, gate, -jnp.inf)
        _, sel = lax.top_k(gate, topk)

    def chunk(c):
        t0 = c * MOBA_Q_CHUNK
        qc = lax.dynamic_slice_in_dim(q, t0, MOBA_Q_CHUNK, axis=2)
        tq = t0 + jnp.arange(MOBA_Q_CHUNK)
        own = t0 // MOBA_BLOCK
        k_own = lax.dynamic_index_in_dim(kb, own, axis=2, keepdims=False)
        v_own = lax.dynamic_index_in_dim(vb, own, axis=2, keepdims=False)
        s_own = jnp.einsum('bhqd,bhkd->bhqk', qc, k_own,
                           preferred_element_type=jnp.float32) * scale
        kpos = own * MOBA_BLOCK + jnp.arange(MOBA_BLOCK)
        s_own = jnp.where(kpos[None, :] <= tq[:, None], s_own, -jnp.inf)
        if topk == 0:
            p_own = jax.nn.softmax(s_own, axis=-1)
            return jnp.einsum('bhqk,bhkd->bhqd', p_own.astype(v.dtype), v_own)
        sel_c = lax.dynamic_slice_in_dim(sel, t0, MOBA_Q_CHUNK, axis=2)
        k_sel = gather_blocks(kb, sel_c)
        v_sel = gather_blocks(vb, sel_c)
        s_sel = jnp.einsum('bhqd,bhqnkd->bhqnk', qc, k_sel,
                           preferred_element_type=jnp.float32) * scale
        valid = sel_c < own
        s_sel = jnp.where(valid[..., None], s_sel, -jnp.inf)
        s_sel = s_sel.reshape(b, h, MOBA_Q_CHUNK, topk * MOBA_BLOCK)
        p = jax.nn.softmax(jnp.concatenate([s_sel, s_own], axis=-1), axis=-1).astype(v.dtype)
        p_sel = p[..., :topk * MOBA_BLOCK].reshape(b, h, MOBA_Q_CHUNK, topk, MOBA_BLOCK)
        p_own = p[..., topk * MOBA_BLOCK:]
        return (jnp.einsum('bhqnk,bhqnkd->bhqd', p_sel, v_sel)
                + jnp.einsum('bhqk,bhkd->bhqd', p_own, v_own))

    outs = lax.map(chunk, jnp.arange(s // MOBA_Q_CHUNK))
    return outs.transpose(1, 2, 0, 3, 4).reshape(b, h, s, d)

def forgetting_attention(q, k, v, log_f):
    b, h, s, d = q.shape
    scale = d ** -0.5
    c = jnp.cumsum(log_f, axis=-1)
    kpos = jnp.arange(s)

    def block(i):
        t0 = i * Q_BLOCK
        qb = lax.dynamic_slice_in_dim(q, t0, Q_BLOCK, axis=2)
        cq = lax.dynamic_slice_in_dim(c, t0, Q_BLOCK, axis=2)
        tq = t0 + jnp.arange(Q_BLOCK)
        sc = (jnp.einsum('bhqd,bhkd->bhqk', qb, k, preferred_element_type=jnp.float32) * scale
              + (cq[..., :, None] - c[..., None, :]))
        sc = jnp.where(kpos[None, :] <= tq[:, None], sc, -jnp.inf)
        p = jax.nn.softmax(sc, axis=-1)
        return jnp.einsum('bhqk,bhkd->bhqd', p.astype(v.dtype), v)

    outs = lax.map(block, jnp.arange(s // Q_BLOCK))
    return outs.transpose(1, 2, 0, 3, 4).reshape(b, h, s, d)

def differential_attention(q1, q2, k1, k2, v, lam):
    b, h, s, d = q1.shape
    scale = d ** -0.5
    kpos = jnp.arange(s)

    def block(i):
        t0 = i * Q_BLOCK
        tq = t0 + jnp.arange(Q_BLOCK)
        mask = kpos[None, :] <= tq[:, None]
        qb1 = lax.dynamic_slice_in_dim(q1, t0, Q_BLOCK, axis=2)
        qb2 = lax.dynamic_slice_in_dim(q2, t0, Q_BLOCK, axis=2)
        s1 = jnp.einsum('bhqd,bhkd->bhqk', qb1, k1, preferred_element_type=jnp.float32) * scale
        s2 = jnp.einsum('bhqd,bhkd->bhqk', qb2, k2, preferred_element_type=jnp.float32) * scale
        p = (jax.nn.softmax(jnp.where(mask, s1, -jnp.inf), axis=-1)
             - lam * jax.nn.softmax(jnp.where(mask, s2, -jnp.inf), axis=-1))
        return jnp.einsum('bhqk,bhkd->bhqd', p.astype(v.dtype), v)

    outs = lax.map(block, jnp.arange(s // Q_BLOCK))
    return outs.transpose(1, 2, 0, 3, 4).reshape(b, h, s, v.shape[-1])

def setup_inputs(seed: int = 0) -> dict:
    key = jax.random.key(seed)
    ks = jax.random.split(key, 20)
    na, nbl, nc = _layers_of(0), _layers_of(1), _layers_of(2)
    f32 = jnp.float32
    w_in_scale = D_MODEL ** -0.5
    w_out_scale = WIDTH ** -0.5

    def gain(k, shape):
        return 1.0 + 0.02 * jax.random.normal(k, shape, f32)

    return {
        "x": jax.random.normal(ks[0], (BATCH, SEQ, D_MODEL), f32),
        "norm_g": gain(ks[1], (DEPTH, D_MODEL)),
        "w_out": jax.random.normal(ks[2], (DEPTH, WIDTH, D_MODEL), f32) * w_out_scale,
        "a_w_in": jax.random.normal(ks[3], (na, D_MODEL, 4 * WIDTH), f32) * w_in_scale,
        "a_q_norm": gain(ks[4], (na, HEAD_DIM)),
        "a_k_norm": gain(ks[5], (na, HEAD_DIM)),
        "b_w_in": jax.random.normal(ks[6], (nbl, D_MODEL, 4 * WIDTH + N_HEADS), f32) * w_in_scale,
        "b_f_bias": jax.random.uniform(ks[7], (nbl, N_HEADS), f32, minval=1.0, maxval=4.0),
        "b_q_norm": gain(ks[8], (nbl, HEAD_DIM)),
        "b_k_norm": gain(ks[9], (nbl, HEAD_DIM)),
        "c_w_in": jax.random.normal(ks[10], (nc, D_MODEL, 4 * WIDTH), f32) * w_in_scale,
        "c_q_norm": gain(ks[11], (nc, DIFF_SUB_DIM)),
        "c_k_norm": gain(ks[12], (nc, DIFF_SUB_DIM)),
        "c_lambda_q1": DIFF_LAMBDA_STD * jax.random.normal(ks[13], (nc, DIFF_SUB_DIM), f32),
        "c_lambda_k1": DIFF_LAMBDA_STD * jax.random.normal(ks[14], (nc, DIFF_SUB_DIM), f32),
        "c_lambda_q2": DIFF_LAMBDA_STD * jax.random.normal(ks[15], (nc, DIFF_SUB_DIM), f32),
        "c_lambda_k2": DIFF_LAMBDA_STD * jax.random.normal(ks[16], (nc, DIFF_SUB_DIM), f32),
        "c_subln": gain(ks[17], (nc, HEAD_DIM)),
    }

def reference(x, norm_g, w_out, a_w_in, a_q_norm, a_k_norm, b_w_in, b_f_bias, b_q_norm, b_k_norm,
              c_w_in, c_q_norm, c_k_norm, c_lambda_q1, c_lambda_k1, c_lambda_q2, c_lambda_k2, c_subln):
    b, s, _ = x.shape
    cos_h, sin_h = rope_tables(s, HEAD_DIM)
    cos_d, sin_d = rope_tables(s, DIFF_SUB_DIM)
    for i in range(DEPTH):
        kind = i % N_MIXERS
        j = i // N_MIXERS
        hdn = rms_norm(x, norm_g[i])
        if kind == 0:
            proj = hdn @ a_w_in[j]
            q, k, v, z = jnp.split(proj, 4, axis=-1)
            q = apply_rope(rms_norm(split_heads(q, N_HEADS), a_q_norm[j]), cos_h, sin_h)
            k = apply_rope(rms_norm(split_heads(k, N_HEADS), a_k_norm[j]), cos_h, sin_h)
            y = moba_attention(q, k, split_heads(v, N_HEADS))
        elif kind == 1:
            proj = hdn @ b_w_in[j]
            q, k, v, z = jnp.split(proj[..., :4 * WIDTH], 4, axis=-1)
            f_logit = (proj[..., 4 * WIDTH:] + b_f_bias[j]).astype(jnp.float32)
            log_f = jax.nn.log_sigmoid(f_logit).transpose(0, 2, 1)
            q = rms_norm(split_heads(q, N_HEADS), b_q_norm[j])
            k = rms_norm(split_heads(k, N_HEADS), b_k_norm[j])
            y = forgetting_attention(q, k, split_heads(v, N_HEADS), log_f)
        else:
            proj = hdn @ c_w_in[j]
            q, k, v, z = jnp.split(proj, 4, axis=-1)
            q = q.reshape(b, s, N_HEADS, 2, DIFF_SUB_DIM).transpose(0, 2, 3, 1, 4)
            k = k.reshape(b, s, N_HEADS, 2, DIFF_SUB_DIM).transpose(0, 2, 3, 1, 4)
            q = apply_rope(rms_norm(q, c_q_norm[j]), cos_d, sin_d)
            k = apply_rope(rms_norm(k, c_k_norm[j]), cos_d, sin_d)
            lambda_init = 0.8 - 0.6 * math.exp(-0.3 * i)
            lam = (jnp.exp(jnp.sum(c_lambda_q1[j] * c_lambda_k1[j]).astype(jnp.float32))
                   - jnp.exp(jnp.sum(c_lambda_q2[j] * c_lambda_k2[j]).astype(jnp.float32))
                   + lambda_init)
            y = differential_attention(q[:, :, 0], q[:, :, 1], k[:, :, 0], k[:, :, 1],
                                       split_heads(v, N_HEADS), lam)
            y = rms_norm(y, c_subln[j]) * (1.0 - lambda_init)
        y = merge_heads(y) * jax.nn.silu(z)
        x = x + y @ w_out[i]
    return x


_drawn_inputs = setup_inputs


def setup_inputs(seed=0):
    import zlib

    import numpy as np

    out = dict(_drawn_inputs(seed))
    spreads = {}
    factors = {'norm_g': 5.593, 'a_q_norm': 8.0, 'a_k_norm': 8.0, 'b_q_norm': 8.0, 'b_k_norm': 8.0}
    for name, (base, spread) in spreads.items():
        noise = np.random.default_rng([zlib.crc32(name.encode()), seed]).standard_normal(out[name].shape)
        drawn = base * np.exp(spread * noise) if base else spread * noise
        out[name] = __import__('jax').numpy.asarray(drawn.astype(out[name].dtype))
    for name, factor in factors.items():
        out[name] = (out[name] * factor).astype(out[name].dtype)
    return out
```

```python
from contextlib import ExitStack

import concourse.bass as bass
import concourse.mybir as mybir

P = 128
SEQ = 512
DM = 1024
HEADS = 8
LAYERS = 2
TILES = SEQ // P
KC = DM // P
CH = SEQ // TILES * 4
OUT_CHUNKS = DM // CH
JOBS = HEADS + OUT_CHUNKS
RAW = 4
EPS = 1e-6
SCALE = float(P) ** -0.5
MASKED = -3.0e38
TRI = sum(P * (t + 1) for t in range(TILES))

F32 = mybir.dt.float32
F32R = mybir.dt.float32r
BF16 = mybir.dt.bfloat16
ALU = mybir.AluOpType
ACT = mybir.ActivationFunctionType
AX = mybir.AxisListType

S_AT = {3: (3, 0), 2: (4, 0), 1: (5, 0), 0: (5, 256)}
T_ORDER = (3, 2, 1, 0)
PT_AT = {0: (3, 0), 1: (4, 0), 2: (5, 0), 3: (5, 256)}
P_COL = {t: sum(P * (u + 1) for u in range(t)) for t in range(TILES)}
PT_COL = {j: sum(SEQ - P * i for i in range(j)) for j in range(TILES)}
PT_GROUPS = ((0,), (1,), (2, 3))


def build_trunk(nc, x, norm_g, w_out, a_w_in, a_q_norm, a_k_norm, b_w_in, b_f_bias, b_q_norm,
                b_k_norm, rope_cos, rope_sin, out):
    with ExitStack() as ctx:
        def sb(name, shape, dt=F32):
            return ctx.enter_context(nc.sbuf_tensor(name, shape, dt))

        def sem(name):
            return ctx.enter_context(nc.semaphore(name))

        xs = sb("xs", [P, TILES, DM])
        hT_hi = sb("hT_hi", [P, KC, SEQ], F32R)
        hT_lo = sb("hT_lo", [P, KC, SEQ], F32R)
        w_raw = sb("w_raw", [P, RAW, CH])
        w_hi = sb("w_hi", [P, 2, KC, CH], F32R)
        w_lo = sb("w_lo", [P, 2, KC, CH], F32R)
        yT_hi = sb("yT_hi", [P, HEADS, SEQ], F32R)
        yT_lo = sb("yT_lo", [P, HEADS, SEQ], F32R)
        qkn = sb("qkn", [P, TILES, 2, P])
        rot = sb("rot", [P, 2, 2, P])
        v_hi = sb("v_hi", [P, 2, TILES, P], F32R)
        v_lo = sb("v_lo", [P, 2, TILES, P], F32R)
        qkT_hi = sb("qkT_hi", [P, 2, SEQ], F32R)
        qkT_lo = sb("qkT_lo", [P, 2, SEQ], F32R)
        probs = sb("probs", [P, TRI])
        pT_hi = sb("pT_hi", [P, TRI], F32R)
        pT_lo = sb("pT_lo", [P, TRI], F32R)
        gz = sb("gz", [P, 2, SEQ])
        cos_t = sb("cos_t", [P, TILES, 2, P])
        sin_t = sb("sin_t", [P, TILES, 2, P])
        crows = sb("crows", [P, SEQ], F32R)
        pick = sb("pick", [P, 2, P], F32R)
        ident = sb("ident", [P, P])
        ident16 = sb("ident16", [P, P], BF16)
        mask16 = sb("mask16", [P, P], BF16)
        junk = sb("junk", [P, 4, P], BF16)
        gains = rot[:, 0]
        onehot = sb("onehot", [P, HEADS])
        wf_raw = rot[:, 1, 0, 0:KC * HEADS].rearrange("p (k h) -> p k h", k=KC)
        wf_hi = sb("wf_hi", [P, KC, HEADS], F32R)
        wf_lo = sb("wf_lo", [P, KC, HEADS], F32R)
        fbias = sb("fbias", [P, HEADS])
        flog = sb("flog", [P, 4, TILES, HEADS])
        ssx = sb("ssx", [P, TILES, 2])
        msx = sb("msx", [P, TILES])
        ssq = sb("ssq", [P, 2, 2])
        msq = sb("msq", [P, 2, 2])
        rstd = sb("rstd", [P, 2, 2])
        power = sb("power", [P, 2])
        eps = sb("eps", [P, 2])
        negmax = sb("negmax", [P, TILES])
        rowsum = sb("rowsum", [P, TILES])
        rinv = sb("rinv", [P, TILES])
        banks = ctx.enter_context(nc.psum_tensor("banks", [P, 8, SEQ], F32))
        Z_BANK, QT_BANK, Y_BANK = 2, 6, 7
        LOGF_BANK, CUM_BANK = 3, 4

        x_in = [sem(f"x_in{t}") for t in range(TILES)]
        small_in = sem("small_in")
        tables_in = sem("tables_in")
        gain_in = [sem(f"gain_in{n}") for n in range(LAYERS)]
        qk_gain_in = sem("qk_gain_in")
        raw_in = [sem(f"raw_in{n}") for n in range(RAW)]
        out_saved = sem("out_saved")
        const_steps = sem("const_steps")
        consts_set = sem("consts_set")
        tables_set = sem("tables_set")
        tri_set = sem("tri_set")
        whi_set = sem("whi_set")
        wlo_set = sem("wlo_set")
        wlo_odd = sem("wlo_odd")
        xsq_set = sem("xsq_set")
        xms_set = sem("xms_set")
        xrs_set = sem("xrs_set")
        xn_set = sem("xn_set")
        hT_turned = sem("hT_turned")
        hThi_set = sem("hThi_set")
        hTlo_set = sem("hTlo_set")
        a_done = sem("a_done")
        ssq_set = sem("ssq_set")
        vhi_set = sem("vhi_set")
        vlo_set = sem("vlo_set")
        msq_set = sem("msq_set")
        rstd_set = sem("rstd_set")
        rot_set = sem("rot_set")
        qkn_set = sem("qkn_set")
        qk_turned = sem("qk_turned")
        qkThi_set = sem("qkThi_set")
        qkTlo_set = sem("qkTlo_set")
        s_done = sem("s_done")
        max_set = sem("max_set")
        exp_set = sem("exp_set")
        rinv_set = sem("rinv_set")
        probs_set = sem("probs_set")
        p_turned = sem("p_turned")
        pThi_set = sem("pThi_set")
        pTlo_set = sem("pTlo_set")
        y_done = sem("y_done")
        y_gated = sem("y_gated")
        yhi_set = sem("yhi_set")
        ylo_set = sem("ylo_set")
        z_done = sem("z_done")
        ez_set = sem("ez_set")
        ez1_set = sem("ez1_set")
        gate_set = sem("gate_set")
        o_done = sem("o_done")
        x_added = sem("x_added")
        f_done = sem("f_done")
        f_step = sem("f_step")
        f_act = sem("f_act")
        cum_done = sem("cum_done")
        wf_split = sem("wf_split")
        chi_set = sem("chi_set")
        c_set = sem("c_set")
        pick_set = sem("pick_set")

        block = ctx.enter_context(nc.Block())

        def wait(eng, s, n):
            if not isinstance(n, int) or n > 0:
                eng.wait_ge(s, n)

        def f32(ap):
            return ap.bitcast(F32)

        def bcast(ap, n):
            return ap.unsqueeze(1).broadcast_to([ap.shape[0], n, ap.shape[1]])

        def normed(layer, t):
            if t == 0 or (layer == 1 and t % 2 == 0):
                return qkn[:, :, :, :].rearrange("p a b n -> p (a b n)")
            return probs[:, 0:DM]

        def heads_loop(eng, layer, first, period, last):
            first(layer)
            period(layer, 0, 0)
            with eng.Fori(0, HEADS // 2 - 1) as i:
                for s in range(2):
                    period(layer, 2 * i + 1 + s, 1 - s)
            last(layer)

        @block.sync
        def _(sp):
            w_in = (a_w_in, b_w_in)

            def load_job(layer, h, src_of, between={}):
                j = JOBS * layer + h
                for k in range(KC):
                    if isinstance(j, int) and j == 0 and k % 2 and k >= RAW:
                        sp.wait_ge(wlo_odd, (k - RAW) // 2 + 1)
                    else:
                        wait(sp, wlo_set, KC * j + k - RAW + 1)
                    dst = w_raw[:, k % RAW, :]
                    src = src_of(k)
                    if len(src.shape) == 3:
                        dst = dst.rearrange("p (g n) -> p g n", n=P)
                    sp.dma_start(dst, src).then_inc(raw_in[k % RAW], 16)
                    if k in between:
                        load, *args = between[k]
                        load(*args)

            def head_src(layer, h):
                def src(k):
                    rows = w_in[layer][0, k * P:(k + 1) * P, 0:4 * DM].rearrange("p (g n) -> p g n", g=4)
                    return rows[:, :, bass.ds(h * P, P)]
                return src

            def out_src(layer, c):
                return lambda k: w_out[layer, k * P:(k + 1) * P, c * CH:(c + 1) * CH]

            def load_x(t):
                sp.dma_start(xs[:, t, :], x[0, t * P:(t + 1) * P, :]).then_inc(x_in[t], 16)

            def load_tables():
                for m in range(2):
                    sp.dma_start(gains[:, m, :], (a_q_norm, a_k_norm)[m][0].partition_broadcast(P)).then_inc(tables_in, 16)
                sp.dma_start(cos_t[:, :, 1, :], rope_cos.rearrange("(t p) n -> p t n", p=P)).then_inc(tables_in, 16)
                sp.dma_start(sin_t[:, :, 1, :], rope_sin.rearrange("(t p) n -> p t n", p=P)).then_inc(tables_in, 16)

            def load_forget():
                sp.dma_start(wf_raw, b_w_in[0, :, 4 * DM:].rearrange("(k p) n -> p k n", p=P)).then_inc(small_in, 16)
                sp.dma_start(fbias[:, :], b_f_bias[0].partition_broadcast(P)).then_inc(small_in, 16)

            load_x(0)
            sp.dma_start(gz[:, :, :].rearrange("p a n -> p (a n)"),
                         norm_g[0].partition_broadcast(P)).then_inc(gain_in[0], 16)
            load_job(0, 0, head_src(0, 0), {1: (load_x, 1), 3: (load_tables,), 4: (load_x, 2),
                                            5: (load_x, 3), 7: (load_forget,)})
            sp.wait_ge(wlo_odd, KC // 2)
            for layer in range(LAYERS):
                with sp.Fori(1 - layer, HEADS) as h:
                    load_job(layer, h, head_src(layer, h))
                for c in range(OUT_CHUNKS):
                    load_job(layer, HEADS + c, out_src(layer, c))
                if layer + 1 < LAYERS:
                    sp.wait_ge(ylo_set, HEADS * (layer + 1))
                    sp.dma_start(gz[:, :, :].rearrange("p a n -> p (a n)"),
                                 norm_g[layer + 1].partition_broadcast(P)).then_inc(gain_in[layer + 1], 16)
                    sp.dma_start(cos_t[:, 0, 0, :], b_q_norm[0].partition_broadcast(P)).then_inc(qk_gain_in, 16)
                    sp.dma_start(cos_t[:, 0, 1, :], b_k_norm[0].partition_broadcast(P)).then_inc(qk_gain_in, 16)
            for t in range(TILES):
                sp.wait_ge(x_added, TILES * OUT_CHUNKS * (LAYERS - 1) + TILES * (OUT_CHUNKS - 1) + t + 1)
                sp.dma_start(out[0, t * P:(t + 1) * P, :], xs[:, t, :]).then_inc(out_saved, 16)
            sp.wait_ge(out_saved, 16 * TILES)

        @block.tensor
        def _(pe):
            def three(dst, pairs, first, last):
                n = len(pairs)
                for m, ((ah, al), (bh, bl)) in enumerate(pairs):
                    pe.matmul(dst, ah, bh, start=first and m == 0, stop=False)
                    pe.matmul(dst, ah, bl, start=False, stop=False)
                    mm = pe.matmul(dst, al, bh, start=False, stop=last and m == n - 1)
                return mm

            def turn_hidden(layer, t):
                n = TILES * layer + t
                buf = normed(layer, t)
                pe.wait_ge(xn_set, n + 1)
                for half in range(2):
                    wait(pe, hTlo_set, 2 * (n - 1) + half + 1)
                    for k in range(4):
                        c = half * 4 + k
                        mm = pe.transpose(banks[:, QT_BANK + half, k * P:(k + 1) * P],
                                          buf[:, c * P:(c + 1) * P], ident[:, :])
                    mm.then_inc(hT_turned, 1)

            def qkv(layer, h, slot, t):
                a = TILES * (HEADS * layer + h) + t
                first_tile = isinstance(a, int) and a == 0
                if t == 0 and not first_tile:
                    wait(pe, wlo_set, KC * (JOBS * layer + h + 1))
                if isinstance(h, int) and h == 0:
                    pe.wait_ge(hTlo_set, 2 * (TILES * layer + t + 1))
                wait(pe, vlo_set, a - 1)
                wait(pe, qkn_set, a - 1)
                for k in range(KC):
                    if first_tile:
                        pe.wait_ge(wlo_odd if k % 2 else wlo_set, k // 2 + 1 if k % 2 else k + 2)
                    mm = three(banks[:, t % 2, 0:3 * P],
                               [((hT_hi[:, k, t * P:(t + 1) * P], hT_lo[:, k, t * P:(t + 1) * P]),
                                 (w_hi[:, slot, k, 0:3 * P], w_lo[:, slot, k, 0:3 * P]))], k == 0, k == KC - 1)
                mm.then_inc(a_done, 1)

            def zproj(layer, h, slot):
                g = HEADS * layer + h
                wait(pe, gate_set, g)
                mm = three(banks[:, Z_BANK, :],
                           [((w_hi[:, slot, k, 3 * P:], w_lo[:, slot, k, 3 * P:]),
                             (hT_hi[:, k, :], hT_lo[:, k, :])) for k in range(KC)], True, True)
                mm.then_inc(z_done, 1)

            def turn_qk(layer, h):
                g = HEADS * layer + h
                pe.wait_ge(qkn_set, TILES * (g + 1))
                wait(pe, qkTlo_set, 2 * g)
                wait(pe, y_gated, g)
                for m in range(2):
                    for t in range(TILES):
                        mm = pe.transpose(banks[:, QT_BANK + m, t * P:(t + 1) * P], qkn[:, t, m, :], ident[:, :])
                    mm.then_inc(qk_turned, 1)

            def scores(layer, h, s):
                g = HEADS * layer + h
                pe.wait_ge(qkTlo_set, 2 * (g + 1))
                wait(pe, pTlo_set, 3 * g)
                if layer == 1:
                    pe.wait_ge(c_set, 1)
                    pe.wait_ge(pick_set, h + 1)
                for t in T_ORDER:
                    bank, col = S_AT[t]
                    w = P * (t + 1)
                    dst = banks[:, bank, col:col + w]
                    rows = slice(t * P, (t + 1) * P)
                    qh, ql = qkT_hi[:, 0, rows], qkT_lo[:, 0, rows]
                    kh, kl = qkT_hi[:, 1, 0:w], qkT_lo[:, 1, 0:w]
                    pe.matmul(dst, qh, kh, start=True, stop=False)
                    pe.matmul(dst, qh, kl, start=False, stop=False)
                    pe.matmul(banks[:, bank, col + t * P:col + w], ident16[:, :], mask16[:, :],
                              start=False, stop=False)
                    if layer == 1:
                        pe.matmul(dst, pick[:, s, :], crows[:, 0:w], start=False, stop=False)
                    mm = pe.matmul(dst, ql, kh, start=False, stop=True)
                    if t != 1:
                        mm.then_inc(s_done, 1)

            def turn_probs(layer, h):
                g = HEADS * layer + h
                pe.wait_ge(probs_set, TILES * (g + 1))
                for js in PT_GROUPS:
                    for j in js:
                        bank, col = PT_AT[j]
                        for t in range(j, TILES):
                            mm = pe.transpose(banks[:, bank, col + (t - j) * P:col + (t - j + 1) * P],
                                              probs[:, P_COL[t] + j * P:P_COL[t] + (j + 1) * P], ident[:, :])
                    mm.then_inc(p_turned, 1)

            def values(layer, h, s):
                g = HEADS * layer + h
                pe.wait_ge(pTlo_set, 3 * (g + 1))
                pe.wait_ge(vlo_set, TILES * (g + 1))
                wait(pe, qkTlo_set, 2 * (g + 1))
                parts = ((v_hi, pT_hi), (v_hi, pT_lo), (v_lo, pT_hi))
                work = [(0, *parts[0]), *((j, *ab) for j in range(1, TILES) for ab in parts),
                        (0, *parts[1]), (0, *parts[2])]
                for n, (j, a, b) in enumerate(work):
                    w = SEQ - j * P
                    mm = pe.matmul(banks[:, Y_BANK, j * P:SEQ], a[:, s, j, :], b[:, PT_COL[j]:PT_COL[j] + w],
                                   start=n == 0, stop=n == len(work) - 1)
                mm.then_inc(y_done, 1)

            def project(layer, c, t, ks, first, last):
                mm = three(banks[:, t, :],
                           [((yT_hi[:, k, t * P:(t + 1) * P], yT_lo[:, k, t * P:(t + 1) * P]),
                             (w_hi[:, c, k, :], w_lo[:, c, k, :])) for k in ks], first, last)
                if last:
                    mm.then_inc(o_done, 1)

            def logf():
                pe.wait_ge(wf_split, 2)
                for t in range(TILES):
                    mm = three(banks[:, LOGF_BANK, t * HEADS:(t + 1) * HEADS],
                               [((hT_hi[:, k, t * P:(t + 1) * P], hT_lo[:, k, t * P:(t + 1) * P]),
                                 (wf_hi[:, k, :], wf_lo[:, k, :])) for k in range(KC)], True, True)
                mm.then_inc(f_done, 1)

            def cumulate():
                pe.wait_ge(f_step, 4)
                pe.wait_ge(tri_set, 2)
                for t in range(TILES):
                    mm = pe.matmul(banks[0:HEADS, CUM_BANK, t * P:SEQ], flog[:, 3, t, :],
                                   sin_t[:, :, :, :].rearrange("p a b n -> p (a b n)")[:, 0:SEQ - t * P],
                                   start=t == 0, stop=t == TILES - 1)
                mm.then_inc(cum_done, 1)

            def first(layer):
                if layer == 0:
                    pe.wait_ge(consts_set, 1)
                    turn_hidden(layer, 0)
                    turn_hidden(layer, 1)
                    for t in range(TILES):
                        qkv(layer, 0, 0, t)
                        if t + 2 < TILES:
                            turn_hidden(layer, t + 2)
                else:
                    qkv(layer, 0, 0, 0)
                    turn_hidden(layer, TILES - 1)
                    for t in range(1, TILES):
                        qkv(layer, 0, 0, t)
                if layer == 1:
                    logf()
                zproj(layer, 0, 0)
                if layer == 1:
                    cumulate()
                turn_qk(layer, 0)

            def period(layer, h, s):
                qkv(layer, h + 1, 1 - s, 0)
                scores(layer, h, s)
                qkv(layer, h + 1, 1 - s, 1)
                qkv(layer, h + 1, 1 - s, 2)
                turn_probs(layer, h)
                qkv(layer, h + 1, 1 - s, 3)
                values(layer, h, s)
                zproj(layer, h + 1, 1 - s)
                turn_qk(layer, h + 1)

            def last(layer):
                g = HEADS * (layer + 1)
                u = TILES * OUT_CHUNKS * layer
                h = HEADS - 1
                head = range(HEADS - 1)
                scores(layer, h, 1)
                pe.wait_ge(wlo_set, KC * (JOBS * layer + HEADS + 1))
                pe.wait_ge(ylo_set, g - 1)
                pe.wait_ge(vlo_set, TILES * g)
                project(layer, 0, 0, head, True, False)
                project(layer, 0, 1, head, True, False)
                turn_probs(layer, h)
                pe.wait_ge(gate_set, g)
                project(layer, 0, 2, head, True, False)
                values(layer, h, 1)
                project(layer, 0, 3, head, True, False)
                pe.wait_ge(ylo_set, g)
                for t in range(TILES):
                    project(layer, 0, t, [h], False, True)
                pe.wait_ge(wlo_set, KC * (JOBS * layer + HEADS + 2))
                for t in range(TILES):
                    pe.wait_ge(x_added, u + 1 + t)
                    project(layer, 1, t, range(HEADS), True, True)
                    if layer + 1 < LAYERS and t >= 1:
                        turn_hidden(layer + 1, t - 1)

            for layer in range(LAYERS):
                heads_loop(pe, layer, first, period, last)

        @block.scalar
        def _(act):
            def split_w(layer, h, slot, ks):
                j = JOBS * layer + h
                for k in ks:
                    if k == 0:
                        if isinstance(h, int) and h < 2:
                            wait(act, o_done, TILES * (OUT_CHUNKS * (layer - 1) + h + 1))
                        else:
                            wait(act, z_done, HEADS * layer + h - 1)
                    wait(act, raw_in[k % RAW], 16 * (2 * j + k // RAW + 1))
                    act.activation(w_hi[:, slot, k, :], w_raw[:, k % RAW, :], ACT.Copy).then_inc(whi_set, 1)

            def square_x(layer, t):
                n = TILES * layer + t
                if layer == 0:
                    act.wait_ge(x_in[t], 16)
                else:
                    act.wait_ge(x_added, TILES * OUT_CHUNKS * layer - TILES + t + 1)
                act.activation(hT_hi[:, :, t * P:(t + 1) * P], xs[:, t, :].rearrange("p (k n) -> p k n", k=KC),
                               ACT.Square, scale=DM ** -0.5, accum_out=ssx[:, t, 0:1]).then_inc(xsq_set, 1)

            def split_hidden(layer, t):
                n = TILES * layer + t
                for half in range(2):
                    act.wait_ge(hT_turned, 2 * n + half + 1)
                    act.activation(hT_hi[:, 4 * half:4 * half + 4, t * P:(t + 1) * P],
                                   banks[:, QT_BANK + half, :].rearrange("p (k n) -> p k n", k=4),
                                   ACT.Copy).then_inc(hThi_set, 1)

            def read_qkv(layer, h, s, t):
                a = TILES * (HEADS * layer + h) + t
                act.wait_ge(a_done, a + 1)
                wait(act, rstd_set, a - 1)
                wait(act, ssq_set, a - 1)
                for m in range(2):
                    sq = act.activation(junk[:, 2 * (t % 2) + m, :], banks[:, t % 2, m * P:(m + 1) * P],
                                        ACT.Square, scale=SCALE, accum_out=ssq[:, t % 2, m:m + 1])
                sq.then_inc(ssq_set, 1)
                act.activation(v_hi[:, s, t, :], banks[:, t % 2, 2 * P:3 * P], ACT.Copy).then_inc(vhi_set, 1)

            def split_qk(layer, h):
                g = HEADS * layer + h
                for m in range(2):
                    act.wait_ge(qk_turned, 2 * g + m + 1)
                    act.activation(qkT_hi[:, m, :], banks[:, QT_BANK + m, :], ACT.Copy).then_inc(qkThi_set, 1)

            def exps(layer, h):
                g = HEADS * layer + h
                wait(act, p_turned, 3 * g)
                for n, t in enumerate(T_ORDER):
                    bank, col = S_AT[t]
                    w = P * (t + 1)
                    act.wait_ge(max_set, TILES * g + (n + 1 if n < 2 else TILES))
                    act.activation(probs[:, P_COL[t]:P_COL[t] + w], banks[:, bank, col:col + w], ACT.Exp,
                                   bias=negmax[:, t:t + 1], accum_out=rowsum[:, t:t + 1]).then_inc(exp_set, 1)

            def split_probs(layer, h):
                g = HEADS * layer + h
                for n, js in enumerate(PT_GROUPS):
                    w = sum(SEQ - j * P for j in js)
                    c = PT_COL[js[0]]
                    act.wait_ge(p_turned, 3 * g + n + 1)
                    act.activation(pT_hi[:, c:c + w], banks[:, PT_AT[js[0]][0], 0:w], ACT.Copy).then_inc(pThi_set, 1)

            def split_y(layer, h):
                g = HEADS * layer + h
                act.wait_ge(y_gated, g + 1)
                act.activation(yT_hi[:, bass.ds(h, 1), :].rearrange("p a n -> p (a n)"), gz[:, 1, :],
                               ACT.Copy).then_inc(yhi_set, 1)

            def exp_z(layer, h):
                g = HEADS * layer + h
                act.wait_ge(z_done, g + 1)
                wait(act, gate_set, g)
                act.activation(gz[:, 0, :], banks[:, Z_BANK, :], ACT.Exp, scale=-1.0).then_inc(ez_set, 1)

            def first(layer):
                if layer == 0:
                    square_x(layer, 0)
                    split_w(layer, 0, 0, (0, 1))
                    square_x(layer, 1)
                    split_hidden(layer, 0)
                    split_w(layer, 0, 0, (2, 3))
                    split_hidden(layer, 1)
                    split_w(layer, 0, 0, (4,))
                    square_x(layer, 2)
                    split_w(layer, 0, 0, (5, 6))
                    square_x(layer, 3)
                    split_w(layer, 0, 0, (7,))
                    act.wait_ge(small_in, 32)
                    act.activation(wf_hi[:, :, :], wf_raw[:, :, :], ACT.Copy).then_inc(wf_split, 1)
                    for t in range(TILES):
                        read_qkv(layer, 0, 0, t)
                        if t + 2 < TILES:
                            split_hidden(layer, t + 2)
                        if t + 1 < TILES:
                            split_w(layer, 1, 1, (2 * t, 2 * t + 1))
                else:
                    read_qkv(layer, 0, 0, 0)
                    split_hidden(layer, TILES - 1)
                    for t in range(1, TILES):
                        split_w(layer, 1, 1, (2 * t - 2, 2 * t - 1))
                        read_qkv(layer, 0, 0, t)
                split_w(layer, 1, 1, (6, 7))
                if layer == 1:
                    act.wait_ge(f_step, 2)
                    act.activation(flog[:, 1, :, :], flog[:, 1, :, :], ACT.Exp, scale=-1.0).then_inc(f_act, 1)
                    act.wait_ge(f_step, 3)
                    act.activation(flog[:, 2, :, :], flog[:, 1, :, :], ACT.Ln).then_inc(f_act, 1)
                exp_z(layer, 0)
                if layer == 1:
                    act.wait_ge(cum_done, 1)
                    act.wait_ge(consts_set, 1)
                    act.activation(crows[0:HEADS, :], banks[0:HEADS, CUM_BANK, :], ACT.Copy,
                                   scale=-1.0).then_inc(chi_set, 1)
                split_qk(layer, 0)

            def period(layer, h, s):
                read_qkv(layer, h + 1, 1 - s, 0)
                exps(layer, h)
                split_w(layer, h + 2, s, (0, 1))
                read_qkv(layer, h + 1, 1 - s, 1)
                split_w(layer, h + 2, s, (2, 3))
                read_qkv(layer, h + 1, 1 - s, 2)
                split_probs(layer, h)
                split_w(layer, h + 2, s, (4, 5, 6, 7))
                read_qkv(layer, h + 1, 1 - s, 3)
                split_y(layer, h)
                split_qk(layer, h + 1)
                exp_z(layer, h + 1)

            def last(layer):
                h = HEADS - 1
                exps(layer, h)
                split_w(layer, h + 2, 1, (0, 1, 2, 3))
                split_probs(layer, h)
                split_y(layer, h)
                split_w(layer, h + 2, 1, (4, 5, 6, 7))
                if layer + 1 < LAYERS:
                    for t in range(TILES):
                        split_w(layer + 1, 0, 0, (2 * t, 2 * t + 1))
                        square_x(layer + 1, t)
                        if t >= 1:
                            split_hidden(layer + 1, t - 1)

            for layer in range(LAYERS):
                heads_loop(act, layer, first, period, last)

        @block.vector
        def _(dve):
            def norm_x(layer, t):
                n = TILES * layer + t
                buf = normed(layer, t)
                dve.wait_ge(xrs_set, n + 1)
                dve.wait_ge(gain_in[layer], 16)
                wait(dve, hT_turned, 2 * (n - 1) if layer else 2 * n * (t > 1))
                dve.scalar_tensor_tensor(out=buf, in0=xs[:, t, :], scalar=ssx[:, t, 1:2],
                                         in1=gz[:, :, :].rearrange("p a n -> p (a n)"),
                                         op0=ALU.mult, op1=ALU.mult).then_inc(xn_set, 1)

            def split_hidden(layer, t):
                n = TILES * layer + t
                for half in range(2):
                    dve.wait_ge(hThi_set, 2 * n + half + 1)
                    dst = slice(4 * half, 4 * half + 4), slice(t * P, (t + 1) * P)
                    dve.tensor_tensor(hT_lo[:, dst[0], dst[1]],
                                      banks[:, QT_BANK + half, :].rearrange("p (k n) -> p k n", k=4),
                                      f32(hT_hi[:, dst[0], dst[1]]), ALU.subtract).then_inc(hTlo_set, 1)

            def split_w_odd(ks):
                for k in ks:
                    dve.wait_ge(whi_set, k + 1)
                    dve.tensor_tensor(w_lo[:, 0, k, :], w_raw[:, k % RAW, :], f32(w_hi[:, 0, k, :]),
                                      ALU.subtract).then_inc(wlo_odd, 1)

            def rope_tables():
                dve.wait_ge(tables_in, 64)
                dve.tensor_scalar(gains[:, 0, :], gains[:, 0, :], SCALE, None, ALU.mult).then_inc(tables_set, 1)
                dve.wait_ge(tables_set, 1)
                half = P // 2
                for m in range(2):
                    dve.tensor_tensor(cos_t[:, :, m, :], cos_t[:, :, 1, :], bcast(gains[:, m, :], TILES), ALU.mult)
                    for a in range(2):
                        last = dve.tensor_tensor(sin_t[:, :, m, a * half:(a + 1) * half],
                                                 sin_t[:, :, 1, a * half:(a + 1) * half],
                                                 bcast(gains[:, m, (1 - a) * half:(2 - a) * half], TILES), ALU.mult)
                last.then_inc(tables_set, 1)

            def rot_steps(layer, h, t):
                return 3 * (TILES * h + t) if layer == 0 else 3 * TILES * HEADS + TILES * h + t

            def read_qkv(layer, h, s, t):
                a = TILES * (HEADS * layer + h) + t
                qk = banks[:, t % 2, 0:2 * P].rearrange("p (m n) -> p m n", m=2)
                r = rot_steps(layer, h, t)
                dve.wait_ge(vhi_set, a + 1)
                wait(dve, qkn_set, a)
                if layer == 0:
                    dve.tensor_tensor(rot[:, 0], qk, cos_t[:, t], ALU.mult).then_inc(rot_set, 1)
                    swapped = banks[:, t % 2, 0:2 * P].rearrange("p (m a n) -> p m a n", m=2, a=2)[:, :, ::-1, :]
                    dve.tensor_tensor(rot[:, 1].rearrange("p m (a n) -> p m a n", a=2), swapped,
                                      sin_t[:, t].rearrange("p m (a n) -> p m a n", a=2), ALU.mult).then_inc(rot_set, 1)
                else:
                    dve.tensor_tensor(rot[:, 0], qk, cos_t[:, 0], ALU.mult).then_inc(rot_set, 1)
                dve.tensor_tensor(v_lo[:, s, t, :], banks[:, t % 2, 2 * P:3 * P], f32(v_hi[:, s, t, :]),
                                  ALU.subtract).then_inc(vlo_set, 1)
                if layer == 0:
                    dve.wait_ge(rot_set, r + 2)
                    dve.tensor_tensor(rot[:, 0], rot[:, 0], rot[:, 1], ALU.add).then_inc(rot_set, 1)

            def norm_qk(layer, h, t):
                a = TILES * (HEADS * layer + h) + t
                dve.wait_ge(rot_set, rot_steps(layer, h, t) + (3 if layer == 0 else 1))
                dve.wait_ge(rstd_set, a + 1)
                for m in range(2):
                    last = dve.tensor_scalar(qkn[:, t, m, :], rot[:, 0, m, :], rstd[:, t % 2, m:m + 1], None, ALU.mult)
                last.then_inc(qkn_set, 1)

            def split_qk(layer, h):
                g = HEADS * layer + h
                for m in range(2):
                    dve.wait_ge(qkThi_set, 2 * g + m + 1)
                    dve.tensor_tensor(qkT_lo[:, m, :], banks[:, QT_BANK + m, :], f32(qkT_hi[:, m, :]),
                                      ALU.subtract).then_inc(qkTlo_set, 1)

            def maxima(layer, h):
                g = HEADS * layer + h
                wait(dve, exp_set, TILES * g)
                for n, t in enumerate(T_ORDER):
                    bank, col = S_AT[t]
                    dve.wait_ge(s_done, 3 * g + min(n, 2) + 1)
                    dve.tensor_reduce(negmax[:, t:t + 1], banks[:, bank, col:col + P * (t + 1)], AX.X, ALU.max,
                                      negate=True).then_inc(max_set, 1)

            def normalise(layer, h):
                g = HEADS * layer + h
                for n, t in enumerate(T_ORDER):
                    dve.wait_ge(exp_set, TILES * g + n + 1)
                    dve.reciprocal(rinv[:, t:t + 1], rowsum[:, t:t + 1]).then_inc(rinv_set, 1)
                for n, t in enumerate(T_ORDER):
                    p = probs[:, P_COL[t]:P_COL[t] + P * (t + 1)]
                    dve.wait_ge(rinv_set, TILES * g + n + 1)
                    dve.tensor_scalar(p, p, rinv[:, t:t + 1], None, ALU.mult).then_inc(probs_set, 1)

            def split_probs(layer, h):
                g = HEADS * layer + h
                for n, js in enumerate(PT_GROUPS):
                    w = sum(SEQ - j * P for j in js)
                    c = PT_COL[js[0]]
                    dve.wait_ge(pThi_set, 3 * g + n + 1)
                    dve.tensor_tensor(pT_lo[:, c:c + w], banks[:, PT_AT[js[0]][0], 0:w], f32(pT_hi[:, c:c + w]),
                                      ALU.subtract).then_inc(pTlo_set, 1)

            def gate_y(layer, h):
                g = HEADS * layer + h
                dve.wait_ge(y_done, g + 1)
                dve.wait_ge(gate_set, g + 1)
                dve.tensor_tensor(gz[:, 1, :], banks[:, Y_BANK, :], gz[:, 1, :], ALU.mult).then_inc(y_gated, 1)
                dve.wait_ge(yhi_set, g + 1)
                row = bass.ds(h, 1)
                dve.tensor_tensor(yT_lo[:, row, :].rearrange("p a n -> p (a n)"), gz[:, 1, :],
                                  f32(yT_hi[:, row, :].rearrange("p a n -> p (a n)")),
                                  ALU.subtract).then_inc(ylo_set, 1)

            def silu(layer, h):
                g = HEADS * layer + h
                dve.wait_ge(ez_set, g + 1)
                dve.tensor_scalar(gz[:, 0, :], gz[:, 0, :], 1.0, None, ALU.add).then_inc(ez1_set, 1)

            def silu_part(layer, h, n):
                g = HEADS * layer + h
                part = gz[:, 0, n * P:(n + 1) * P]
                if n == 0:
                    dve.wait_ge(ez1_set, 5 * g + 1)
                dve.reciprocal(part, part).then_inc(ez1_set, 1)
                if n == 3:
                    dve.wait_ge(ez1_set, 5 * g + 5)
                    wait(dve, ylo_set, g)
                    dve.tensor_tensor(gz[:, 1, :], banks[:, Z_BANK, :], gz[:, 0, :], ALU.mult).then_inc(gate_set, 1)

            def set_pick(h, s):
                wait(dve, s_done, 3 * (HEADS + h - 1))
                dve.tensor_scalar(pick[:, s, :], ident[:, :], 0.0, onehot[:, bass.ds(h, 1)],
                                  ALU.mult, ALU.add).then_inc(pick_set, 1)

            def add_unit(layer, u):
                c, t = divmod(u, TILES)
                n = TILES * OUT_CHUNKS * layer + u
                dve.wait_ge(o_done, n + 1)
                part = xs[:, t, c * CH:(c + 1) * CH]
                dve.tensor_tensor(part, banks[:, t, :], part, ALU.add).then_inc(x_added, 1)

            def log_sigmoid():
                f, e, ln, lf = (flog[:, n] for n in range(4))
                dve.wait_ge(f_done, 1)
                dve.tensor_tensor(f, banks[:, LOGF_BANK, 0:TILES * HEADS].rearrange("p (t h) -> p t h", t=TILES),
                                  bcast(fbias[:, :], TILES), ALU.add).then_inc(f_step, 1)
                dve.wait_ge(f_step, 1)
                dve.scalar_tensor_tensor(out=e, in0=f, scalar=-1.0, in1=f, op0=ALU.mult,
                                         op1=ALU.max).then_inc(f_step, 1)
                dve.wait_ge(f_act, 1)
                dve.tensor_scalar(e, e, 1.0, None, ALU.add).then_inc(f_step, 1)
                dve.wait_ge(f_act, 2)
                dve.scalar_tensor_tensor(out=lf, in0=f, scalar=0.0, in1=ln, op0=ALU.min,
                                         op1=ALU.subtract).then_inc(f_step, 1)

            def first(layer):
                if layer == 0:
                    norm_x(layer, 0)
                    split_w_odd((1,))
                    norm_x(layer, 1)
                    split_hidden(layer, 0)
                    split_w_odd((3,))
                    split_hidden(layer, 1)
                    rope_tables()
                    split_w_odd((5, 7))
                    norm_x(layer, 2)
                    dve.wait_ge(small_in, 32)
                    dve.wait_ge(wf_split, 1)
                    dve.tensor_tensor(wf_lo[:, :, :], wf_raw[:, :, :], f32(wf_hi[:, :, :]),
                                      ALU.subtract).then_inc(wf_split, 1)
                    dve.wait_ge(wf_split, 2)
                    dve.wait_ge(tables_set, 2)
                    for t in range(TILES):
                        read_qkv(layer, 0, 0, t)
                        if t + 2 < TILES:
                            split_hidden(layer, t + 2)
                        if t == 0:
                            norm_x(layer, 3)
                        norm_qk(layer, 0, t)
                else:
                    dve.wait_ge(qk_gain_in, 32)
                    dve.tensor_scalar(cos_t[:, 0, 0, :], cos_t[:, 0, 0, :], SCALE, None, ALU.mult).then_inc(tables_set, 1)
                    dve.wait_ge(tables_set, 3)
                    read_qkv(layer, 0, 0, 0)
                    norm_qk(layer, 0, 0)
                    split_hidden(layer, TILES - 1)
                    for t in range(1, TILES):
                        read_qkv(layer, 0, 0, t)
                        norm_qk(layer, 0, t)
                    log_sigmoid()
                    dve.wait_ge(consts_set, 1)
                    set_pick(0, 0)
                if layer == 1:
                    dve.wait_ge(chi_set, 1)
                    dve.scalar_tensor_tensor(out=crows[32:32 + HEADS, :], in0=banks[0:HEADS, CUM_BANK, :], scalar=-1.0,
                                             in1=f32(crows[0:HEADS, :]), op0=ALU.mult,
                                             op1=ALU.subtract).then_inc(c_set, 1)
                split_qk(layer, 0)

            def period(layer, h, s):
                read_qkv(layer, h + 1, 1 - s, 0)
                silu(layer, h)
                norm_qk(layer, h + 1, 0)
                maxima(layer, h)
                silu_part(layer, h, 0)
                normalise(layer, h)
                read_qkv(layer, h + 1, 1 - s, 1)
                silu_part(layer, h, 1)
                silu_part(layer, h, 2)
                norm_qk(layer, h + 1, 1)
                split_probs(layer, h)
                silu_part(layer, h, 3)
                read_qkv(layer, h + 1, 1 - s, 2)
                norm_qk(layer, h + 1, 2)
                read_qkv(layer, h + 1, 1 - s, 3)
                gate_y(layer, h)
                norm_qk(layer, h + 1, 3)
                if layer == 1:
                    set_pick(h + 1, 1 - s)
                split_qk(layer, h + 1)

            def last(layer):
                h = HEADS - 1
                silu(layer, h)
                maxima(layer, h)
                silu_part(layer, h, 0)
                normalise(layer, h)
                for n in range(1, 4):
                    silu_part(layer, h, n)
                split_probs(layer, h)
                gate_y(layer, h)
                for u in range(TILES * OUT_CHUNKS):
                    add_unit(layer, u)
                    t = u - TILES
                    if layer + 1 < LAYERS and t >= 0:
                        norm_x(layer + 1, t)
                        if t >= 1:
                            split_hidden(layer + 1, t - 1)

            for layer in range(LAYERS):
                heads_loop(dve, layer, first, period, last)

        @block.gpsimd
        def _(pool):
            def split_w(layer, h, slot, ks, by=1):
                j = JOBS * layer + h
                for k in ks:
                    wait(pool, whi_set, KC * j + k + 1)
                    pool.tensor_tensor(w_lo[:, slot, k, :], w_raw[:, k % RAW, :], f32(w_hi[:, slot, k, :]),
                                       ALU.subtract).then_inc(wlo_set, by)

            def rstd_x(layer, t):
                n = TILES * layer + t
                pool.wait_ge(xsq_set, n + 1)
                pool.tensor_tensor(msx[:, t:t + 1], ssx[:, t, 0:1], eps[:, 0:1], ALU.add).then_inc(xms_set, 1)
                pool.wait_ge(xms_set, n + 1)
                pool.tensor_tensor(ssx[:, t, 1:2], msx[:, t:t + 1], power[:, 0:1],
                                   ALU.pow).then_inc(xrs_set, 1)

            def rstd_qk(layer, h, t):
                a = TILES * (HEADS * layer + h) + t
                pool.wait_ge(ssq_set, a + 1)
                wait(pool, qkn_set, a - 1)
                pool.tensor_tensor(msq[:, t % 2, :], ssq[:, t % 2, :], eps[:, :], ALU.add).then_inc(msq_set, 1)
                pool.wait_ge(msq_set, a + 1)
                pool.tensor_tensor(rstd[:, t % 2, :], msq[:, t % 2, :], power[:, :], ALU.pow).then_inc(rstd_set, 1)

            pool.memset(ident[:, :], 0.0)
            pool.memset(ident16[:, :], 0.0)
            pool.memset(mask16[:, :], 0.0)
            pool.memset(onehot[:, :], 0.0)
            pool.memset(f32(crows[:, :]), 0.0)
            pool.memset(eps[:, :], EPS)
            pool.memset(power[:, :], -0.5).then_inc(const_steps, 1)
            pool.wait_ge(const_steps, 1)
            for m in (ident, ident16):
                pool.affine_select(out=m[:, :], in_=m[:, :], compare_op=ALU.not_equal, fill=1.0, base=0,
                                   pattern=[[-1, P]], channel_multiplier=1)
            pool.affine_select(out=mask16[:, :], in_=mask16[:, :], compare_op=ALU.is_ge, fill=MASKED, base=0,
                               pattern=[[-1, P]], channel_multiplier=1)
            pool.affine_select(out=onehot[:, :], in_=onehot[:, :], compare_op=ALU.not_equal, fill=1.0, base=0,
                               pattern=[[-1, HEADS]], channel_multiplier=1).then_inc(const_steps, 1)
            pool.wait_ge(const_steps, 2)
            pool.affine_select(out=onehot[:, :], in_=onehot[:, :], compare_op=ALU.not_equal, fill=1.0, base=-32,
                               pattern=[[-1, HEADS]], channel_multiplier=1).then_inc(consts_set, 1)
            pool.wait_ge(consts_set, 1)

            def first(layer):
                if layer == 0:
                    rstd_x(layer, 0)
                    split_w(layer, 0, 0, (0,), by=2)
                    rstd_x(layer, 1)
                    split_w(layer, 0, 0, (2,), by=2)
                    split_w(layer, 0, 0, (4,), by=2)
                    rstd_x(layer, 2)
                    split_w(layer, 0, 0, (6,), by=2)
                    rstd_x(layer, 3)
                else:
                    tri = sin_t[:, :, :, :].rearrange("p a b n -> p (a b n)")[:, 0:SEQ]
                    pool.wait_ge(qkn_set, TILES * HEADS)
                    pool.memset(tri, 1.0).then_inc(tri_set, 1)
                    pool.wait_ge(tri_set, 1)
                    pool.affine_select(out=tri, in_=tri, compare_op=ALU.is_ge, fill=0.0, base=0,
                                       pattern=[[1, SEQ]], channel_multiplier=-1).then_inc(tri_set, 1)
                rstd_qk(layer, 0, 0)
                for t in range(1, TILES):
                    split_w(layer, 1, 1, (2 * t - 2, 2 * t - 1))
                    rstd_qk(layer, 0, t)
                split_w(layer, 1, 1, (6, 7))

            def period(layer, h, s):
                rstd_qk(layer, h + 1, 0)
                split_w(layer, h + 2, s, (0, 1))
                rstd_qk(layer, h + 1, 1)
                split_w(layer, h + 2, s, (2, 3))
                rstd_qk(layer, h + 1, 2)
                split_w(layer, h + 2, s, (4, 5, 6, 7))
                rstd_qk(layer, h + 1, 3)

            def last(layer):
                split_w(layer, HEADS + 1, 1, range(KC))
                if layer + 1 < LAYERS:
                    for t in range(TILES):
                        split_w(layer + 1, 0, 0, (2 * t, 2 * t + 1))
                        rstd_x(layer + 1, t)

            for layer in range(LAYERS):
                heads_loop(pool, layer, first, period, last)


_INS = ["x", "norm_g", "w_out", "a_w_in", "a_q_norm", "a_k_norm", "b_w_in", "b_f_bias", "b_q_norm", "b_k_norm"]
_OUT = ((1, SEQ, DM), "float32")


def rope_constants():
    import numpy as np

    half = P // 2
    inv = 1.0 / np.float32(10000.0) ** (np.arange(0, P, 2, dtype=np.float32) / np.float32(P))
    ang = np.arange(SEQ, dtype=np.float32)[:, None] * inv.astype(np.float32)[None, :]
    cos, sin = np.cos(ang).astype(np.float32), np.sin(ang).astype(np.float32)
    assert cos.shape == (SEQ, half)
    return np.concatenate([cos, cos], 1), np.concatenate([-sin, sin], 1)


def kernel(**inputs):
    import numpy as np
    import concourse.bacc as bacc
    from concourse.bass_utils import run_bass_kernel_spmd

    nc = bacc.Bacc("TRN2", target_bir_lowering=False, num_devices=1)
    given = {name: np.ascontiguousarray(inputs[name]) for name in _INS}
    given["rope_cos"], given["rope_sin"] = rope_constants()
    arrays, args = {}, []
    for name, a in given.items():
        arrays[f"in_{name}_dram"] = a
        args.append(nc.dram_tensor(f"in_{name}_dram", a.shape, mybir.dt.from_np(a.dtype), kind="ExternalInput").ap())
    shape, dtype = _OUT
    args.append(nc.dram_tensor("out_0_dram", shape, mybir.dt.from_np(np.dtype(dtype)), kind="ExternalOutput").ap())
    build_trunk(nc, *args)
    r = run_bass_kernel_spmd(nc, [arrays], core_ids=[0])
    return r.results[0]["out_0_dram"]
```

```python
from contextlib import ExitStack

import concourse.bass as bass
import concourse.mybir as mybir

P = 128
SEQ = 512
DM = 1024
HEADS = 8
LAYERS = 2
TILES = SEQ // P
KC = DM // P
CH = 4 * P
OUT_CHUNKS = DM // CH
JOBS = HEADS + OUT_CHUNKS
WARM_UPS = 19
RAW = 4
EPS = 1e-6
SCALE = float(P) ** -0.5
MASKED = -3.0e38
TRI = sum(P * (t + 1) for t in range(TILES))

F32 = mybir.dt.float32
F32R = mybir.dt.float32r
BF16 = mybir.dt.bfloat16
ALU = mybir.AluOpType
ACT = mybir.ActivationFunctionType
AX = mybir.AxisListType

S_AT = {3: (3, 0), 2: (4, 0), 1: (5, 0), 0: (5, 256)}
T_ORDER = (3, 2, 1, 0)
PT_AT = {0: (3, 0), 1: (4, 0), 2: (5, 0), 3: (5, 256)}
P_COL = {t: sum(P * (u + 1) for u in range(t)) for t in range(TILES)}
PT_COL = {j: sum(SEQ - P * i for i in range(j)) for j in range(TILES)}
PT_GROUPS = ((0,), (1,), (2, 3))


def build_trunk(nc, x, norm_g, w_out, a_w_in, a_q_norm, a_k_norm, b_w_in, b_f_bias, b_q_norm,
                b_k_norm, rope_cos, rope_sin, out):
    with ExitStack() as ctx:
        def sb(name, shape, dt=F32):
            return ctx.enter_context(nc.sbuf_tensor(name, shape, dt))

        def sem(name):
            return ctx.enter_context(nc.semaphore(name))

        xs = sb("xs", [P, TILES, DM])
        hT_hi = sb("hT_hi", [P, KC, SEQ], F32R)
        hT_lo = sb("hT_lo", [P, KC, SEQ], F32R)
        w_raw = sb("w_raw", [P, RAW, CH])
        w_hi = sb("w_hi", [P, 2, KC, CH], F32R)
        w_lo = sb("w_lo", [P, 2, KC, CH], F32R)
        with nc.sbuf_tensor("first_raw", [P, KC, CH], F32) as first_raw, \
             nc.sbuf_tensor("wf_raw", [P, KC, HEADS], F32) as wf_raw, \
             nc.sbuf_tensor("gains", [P, 2, P], F32) as gains, \
             nc.sbuf_tensor("xn_2", [P, DM], F32) as xn_2:
            pass
        yT_hi = sb("yT_hi", [P, HEADS, SEQ], F32R)
        yT_lo = sb("yT_lo", [P, HEADS, SEQ], F32R)
        qkn = sb("qkn", [P, TILES, 2, P])
        rot = sb("rot", [P, 2, 2, P])
        v_hi = sb("v_hi", [P, 2, TILES, P], F32R)
        v_lo = sb("v_lo", [P, 2, TILES, P], F32R)
        qkT_hi = sb("qkT_hi", [P, 2, SEQ], F32R)
        qkT_lo = sb("qkT_lo", [P, 2, SEQ], F32R)
        probs = sb("probs", [P, TRI])
        pT_hi = sb("pT_hi", [P, TRI], F32R)
        pT_lo = sb("pT_lo", [P, TRI], F32R)
        gz = sb("gz", [P, 2, SEQ])
        cos_t = sb("cos_t", [P, TILES, 2, P])
        sin_t = sb("sin_t", [P, TILES, 2, P])
        crows = sb("crows", [P, SEQ], F32R)
        pick = sb("pick", [P, 2, P], F32R)
        ident = sb("ident", [P, P])
        mask = sb("mask", [P, P])
        junk = sb("junk", [P, 4, P], BF16)
        onehot = sb("onehot", [P, HEADS])
        wf_hi = sb("wf_hi", [P, KC, HEADS], F32R)
        wf_lo = sb("wf_lo", [P, KC, HEADS], F32R)
        fbias = sb("fbias", [P, HEADS])
        flog = sb("flog", [P, 4, TILES, HEADS])
        ssx = sb("ssx", [P, TILES, 2])
        msx = sb("msx", [P, TILES])
        ssq = sb("ssq", [P, 2, 2])
        msq = sb("msq", [P, 2, 2])
        rstd = sb("rstd", [P, 2, 2])
        power = sb("power", [P, 2])
        eps = sb("eps", [P, 2])
        negmax = sb("negmax", [P, TILES])
        rowsum = sb("rowsum", [P, TILES])
        rinv = sb("rinv", [P, TILES])
        banks = ctx.enter_context(nc.psum_tensor("banks", [P, 8, SEQ], F32))
        Z_BANK, QT_BANK, Y_BANK = 2, 6, 7
        LOGF_BANK, CUM_BANK = 3, 4

        x_in = [sem(f"x_in{t}") for t in range(TILES)]
        small_in = sem("small_in")
        tables_in = sem("tables_in")
        gain_in = [sem(f"gain_in{n}") for n in range(LAYERS)]
        qk_gain_in = sem("qk_gain_in")
        first_in = [sem(f"first_in{k}") for k in range(KC)]
        raw_in = [sem(f"raw_in{n}") for n in range(RAW)]
        out_saved = sem("out_saved")
        const_steps = sem("const_steps")
        consts_set = sem("consts_set")
        tables_set = sem("tables_set")
        tri_set = sem("tri_set")
        whi_set = sem("whi_set")
        wlo_set = sem("wlo_set")
        wlo_odd = sem("wlo_odd")
        xsq_set = sem("xsq_set")
        xms_set = sem("xms_set")
        xrs_set = sem("xrs_set")
        xn_set = sem("xn_set")
        hT_turned = sem("hT_turned")
        hThi_set = sem("hThi_set")
        hTlo_set = sem("hTlo_set")
        a_done = sem("a_done")
        ssq_set = sem("ssq_set")
        vhi_set = sem("vhi_set")
        vlo_set = sem("vlo_set")
        msq_set = sem("msq_set")
        rstd_set = sem("rstd_set")
        rot_set = sem("rot_set")
        qkn_set = sem("qkn_set")
        qk_turned = sem("qk_turned")
        qkThi_set = sem("qkThi_set")
        qkTlo_set = sem("qkTlo_set")
        s_done = sem("s_done")
        mask_added = sem("mask_added")
        max_set = sem("max_set")
        exp_set = sem("exp_set")
        rinv_set = sem("rinv_set")
        probs_set = sem("probs_set")
        p_turned = sem("p_turned")
        pThi_set = sem("pThi_set")
        pTlo_set = sem("pTlo_set")
        y_done = sem("y_done")
        y_gated = sem("y_gated")
        yhi_set = sem("yhi_set")
        ylo_set = sem("ylo_set")
        z_done = sem("z_done")
        ez_set = sem("ez_set")
        ez1_set = sem("ez1_set")
        gate_set = sem("gate_set")
        o_done = sem("o_done")
        x_added = sem("x_added")
        f_done = sem("f_done")
        f_step = sem("f_step")
        f_act = sem("f_act")
        cum_done = sem("cum_done")
        wf_split = sem("wf_split")
        chi_set = sem("chi_set")
        c_set = sem("c_set")
        pick_set = sem("pick_set")

        block = ctx.enter_context(nc.Block())

        def wait(eng, s, n):
            if not isinstance(n, int) or n > 0:
                eng.wait_ge(s, n)

        def f32(ap):
            return ap.bitcast(F32)

        def bcast(ap, n):
            return ap.unsqueeze(1).broadcast_to([ap.shape[0], n, ap.shape[1]])

        def unit_bank(c, t):
            return QT_BANK if c == 0 and t == 3 else t

        out_parts = [(unit_bank(c, t), t, slice(c * CH, (c + 1) * CH)) for c in range(OUT_CHUNKS) for t in range(TILES)]
        bank, t, cols = out_parts.pop()
        out_parts += [(bank, t, slice(cols.start, cols.start + CH // 2)),
                      (QT_BANK, t, slice(cols.start + CH // 2, cols.stop))]

        def normed(layer, t):
            if layer == 0 and t == 2:
                return xn_2[:, :]
            if t == 0 or (layer == 1 and t % 2 == 0):
                return qkn[:, :, :, :].rearrange("p a b n -> p (a b n)")
            return probs[:, 0:DM]

        def heads_loop(eng, layer, first, period, last):
            first(layer)
            period(layer, 0, 0)
            with eng.Fori(0, HEADS // 2 - 1) as i:
                for s in range(2):
                    period(layer, 2 * i + 1 + s, 1 - s)
            last(layer)

        @block.sync
        def _(sp):
            w_in = (a_w_in, b_w_in)

            def load_job(layer, h, src_of):
                j = JOBS * layer + h
                for k in range(KC):
                    if not isinstance(j, int) or j > 1 or k >= RAW:
                        sp.wait_ge(wlo_set, KC * j + k - RAW + 1)
                    load_chunk(w_raw[:, k % RAW, :], src_of(k), raw_in[k % RAW])

            def load_chunk(dst, src, loaded):
                if len(src.shape) == 3:
                    dst = dst.rearrange("p (g n) -> p g n", n=P)
                sp.dma_start(dst, src).then_inc(loaded, 16)

            def load_first(ks):
                for k in ks:
                    load_chunk(first_raw[:, k, :], head_src(0, 0)(k), first_in[k])

            def head_src(layer, h):
                def src(k):
                    rows = w_in[layer][0, k * P:(k + 1) * P, 0:4 * DM].rearrange("p (g n) -> p g n", g=4)
                    return rows[:, :, bass.ds(h * P, P)]
                return src

            def out_src(layer, c):
                return lambda k: w_out[layer, k * P:(k + 1) * P, c * CH:(c + 1) * CH]

            def load_x(t):
                sp.dma_start(xs[:, t, :], x[0, t * P:(t + 1) * P, :]).then_inc(x_in[t], 16)

            def load_tables():
                for m in range(2):
                    sp.dma_start(gains[:, m, :], (a_q_norm, a_k_norm)[m][0].partition_broadcast(P)).then_inc(tables_in, 16)
                sp.dma_start(cos_t[:, :, 1, :], rope_cos.rearrange("(t p) n -> p t n", p=P)).then_inc(tables_in, 16)
                sp.dma_start(sin_t[:, :, 1, :], rope_sin.rearrange("(t p) n -> p t n", p=P)).then_inc(tables_in, 16)

            def load_forget():
                sp.dma_start(wf_raw[:, :, :], b_w_in[0, :, 4 * DM:].rearrange("(k p) n -> p k n", p=P)).then_inc(small_in, 16)
                sp.dma_start(fbias[:, :], b_f_bias[0].partition_broadcast(P)).then_inc(small_in, 16)

            load_x(0)
            sp.dma_start(gz[:, :, :].rearrange("p a n -> p (a n)"),
                         norm_g[0].partition_broadcast(P)).then_inc(gain_in[0], 16)
            load_first(range(0, 4))
            load_x(1)
            load_first(range(4, 6))
            load_x(2)
            load_first(range(6, KC))
            load_tables()
            load_x(3)
            load_forget()
            load_job(0, 1, head_src(0, 1))
            for layer in range(LAYERS):
                with sp.Fori(0 if layer else 2, HEADS) as h:
                    load_job(layer, h, head_src(layer, h))
                for c in range(OUT_CHUNKS):
                    load_job(layer, HEADS + c, out_src(layer, c))
                if layer + 1 < LAYERS:
                    sp.wait_ge(ylo_set, HEADS * (layer + 1))
                    sp.dma_start(gz[:, :, :].rearrange("p a n -> p (a n)"),
                                 norm_g[layer + 1].partition_broadcast(P)).then_inc(gain_in[layer + 1], 16)
                    sp.dma_start(cos_t[:, 0, 0, :], b_q_norm[0].partition_broadcast(P)).then_inc(qk_gain_in, 16)
                    sp.dma_start(cos_t[:, 0, 1, :], b_k_norm[0].partition_broadcast(P)).then_inc(qk_gain_in, 16)
            for n, (_, t, cols) in enumerate(out_parts):
                sp.wait_ge(x_added, TILES * OUT_CHUNKS * (LAYERS - 1) + n + 1)
                sp.dma_start(out[0, t * P:(t + 1) * P, cols], xs[:, t, cols]).then_inc(out_saved, 16)
            sp.wait_ge(out_saved, 16 * len(out_parts))

        @block.tensor
        def _(pe):
            def three(dst, pairs, first, last):
                n = len(pairs)
                for m, ((ah, al), (bh, bl)) in enumerate(pairs):
                    pe.matmul(dst, ah, bh, start=first and m == 0, stop=False)
                    pe.matmul(dst, ah, bl, start=False, stop=False)
                    mm = pe.matmul(dst, al, bh, start=False, stop=last and m == n - 1)
                return mm

            def warm_up():
                for _ in range(WARM_UPS):
                    pe.transpose(banks[:, Y_BANK, 0:P], ident[:, :], ident[:, :])

            def turn_hidden(layer, t):
                n = TILES * layer + t
                buf = normed(layer, t)
                for half in range(2):
                    pe.wait_ge(xn_set, 2 * n + half + 1)
                    wait(pe, hTlo_set, 2 * (n - 1) + half + 1)
                    for k in range(4):
                        c = half * 4 + k
                        mm = pe.transpose(banks[:, QT_BANK + half, k * P:(k + 1) * P],
                                          buf[:, c * P:(c + 1) * P], ident[:, :])
                    mm.then_inc(hT_turned, 1)

            def qkv(layer, h, slot, t, halfway=None):
                a = TILES * (HEADS * layer + h) + t
                first_tile = isinstance(a, int) and a == 0
                if t == 0 and not first_tile:
                    wait(pe, wlo_set, KC * (JOBS * layer + h + 1))
                wait(pe, vlo_set, a - 1)
                for k in range(KC):
                    if k == KC // 2 and halfway:
                        halfway()
                    if isinstance(h, int) and h == 0 and k % 4 == 0:
                        pe.wait_ge(hTlo_set, 2 * (TILES * layer + t) + k // 4 + 1)
                    if first_tile:
                        pe.wait_ge(wlo_odd if k % 2 else wlo_set, k // 2 + 1 if k % 2 else k + 2)
                    mm = three(banks[:, t % 2, 0:3 * P],
                               [((hT_hi[:, k, t * P:(t + 1) * P], hT_lo[:, k, t * P:(t + 1) * P]),
                                 (w_hi[:, slot, k, 0:3 * P], w_lo[:, slot, k, 0:3 * P]))], k == 0, k == KC - 1)
                mm.then_inc(a_done, 1)

            def zproj(layer, h, slot):
                g = HEADS * layer + h
                wait(pe, gate_set, g)
                mm = three(banks[:, Z_BANK, :],
                           [((w_hi[:, slot, k, 3 * P:], w_lo[:, slot, k, 3 * P:]),
                             (hT_hi[:, k, :], hT_lo[:, k, :])) for k in range(KC)], True, True)
                mm.then_inc(z_done, 1)

            def turn_qk(layer, h):
                g = HEADS * layer + h
                pe.wait_ge(qkn_set, TILES * (g + 1))
                wait(pe, qkTlo_set, 2 * g)
                wait(pe, y_gated, g)
                for m in range(2):
                    for t in range(TILES):
                        mm = pe.transpose(banks[:, QT_BANK + m, t * P:(t + 1) * P], qkn[:, t, m, :], ident[:, :])
                    mm.then_inc(qk_turned, 1)

            def scores(layer, h, s):
                g = HEADS * layer + h
                pe.wait_ge(qkTlo_set, 2 * (g + 1))
                wait(pe, pTlo_set, 3 * g)
                if layer == 1:
                    pe.wait_ge(c_set, 1)
                    pe.wait_ge(pick_set, h + 1)
                for t in T_ORDER:
                    bank, col = S_AT[t]
                    w = P * (t + 1)
                    dst = banks[:, bank, col:col + w]
                    rows = slice(t * P, (t + 1) * P)
                    qh, ql = qkT_hi[:, 0, rows], qkT_lo[:, 0, rows]
                    kh, kl = qkT_hi[:, 1, 0:w], qkT_lo[:, 1, 0:w]
                    pe.matmul(dst, qh, kh, start=True, stop=False)
                    pe.matmul(dst, qh, kl, start=False, stop=False)
                    if layer == 1:
                        pe.matmul(dst, pick[:, s, :], crows[:, 0:w], start=False, stop=False)
                    mm = pe.matmul(dst, ql, kh, start=False, stop=True)
                    if t != 1:
                        mm.then_inc(s_done, 1)

            def turn_probs(layer, h):
                g = HEADS * layer + h
                pe.wait_ge(probs_set, TILES * (g + 1))
                for js in PT_GROUPS:
                    for j in js:
                        bank, col = PT_AT[j]
                        for t in range(j, TILES):
                            mm = pe.transpose(banks[:, bank, col + (t - j) * P:col + (t - j + 1) * P],
                                              probs[:, P_COL[t] + j * P:P_COL[t] + (j + 1) * P], ident[:, :])
                    mm.then_inc(p_turned, 1)

            def values(layer, h, s):
                g = HEADS * layer + h
                pe.wait_ge(pTlo_set, 3 * (g + 1))
                pe.wait_ge(vlo_set, TILES * (g + 1))
                wait(pe, qkTlo_set, 2 * (g + 1))
                parts = ((v_hi, pT_hi), (v_hi, pT_lo), (v_lo, pT_hi))
                work = [(0, *parts[0]), *((j, *ab) for j in range(1, TILES) for ab in parts),
                        (0, *parts[1]), (0, *parts[2])]
                for n, (j, a, b) in enumerate(work):
                    w = SEQ - j * P
                    mm = pe.matmul(banks[:, Y_BANK, j * P:SEQ], a[:, s, j, :], b[:, PT_COL[j]:PT_COL[j] + w],
                                   start=n == 0, stop=n == len(work) - 1)
                mm.then_inc(y_done, 1)

            def project(layer, c, t, ks, first, last):
                mm = three(banks[:, unit_bank(c, t), :],
                           [((yT_hi[:, k, t * P:(t + 1) * P], yT_lo[:, k, t * P:(t + 1) * P]),
                             (w_hi[:, c, k, :], w_lo[:, c, k, :])) for k in ks], first, last)
                if last:
                    mm.then_inc(o_done, 1)

            def project_part(bank, t, cols):
                w = slice(cols.start - CH, cols.stop - CH)
                mm = three(banks[:, bank, 0:w.stop - w.start],
                           [((yT_hi[:, k, t * P:(t + 1) * P], yT_lo[:, k, t * P:(t + 1) * P]),
                             (w_hi[:, 1, k, w], w_lo[:, 1, k, w])) for k in range(HEADS)], True, True)
                mm.then_inc(o_done, 1)

            def logf():
                pe.wait_ge(wf_split, 2)
                for t in range(TILES):
                    mm = three(banks[:, LOGF_BANK, t * HEADS:(t + 1) * HEADS],
                               [((hT_hi[:, k, t * P:(t + 1) * P], hT_lo[:, k, t * P:(t + 1) * P]),
                                 (wf_hi[:, k, :], wf_lo[:, k, :])) for k in range(KC)], True, True)
                mm.then_inc(f_done, 1)

            def cumulate():
                pe.wait_ge(f_step, 4)
                pe.wait_ge(tri_set, 2)
                for t in range(TILES):
                    mm = pe.matmul(banks[0:HEADS, CUM_BANK, t * P:SEQ], flog[:, 3, t, :],
                                   sin_t[:, :, :, :].rearrange("p a b n -> p (a b n)")[:, 0:SEQ - t * P],
                                   start=t == 0, stop=t == TILES - 1)
                mm.then_inc(cum_done, 1)

            def first(layer):
                if layer == 0:
                    pe.wait_ge(consts_set, 1)
                    warm_up()
                    turn_hidden(layer, 0)
                    for t in range(TILES):
                        qkv(layer, 0, 0, t, (lambda: turn_hidden(layer, t + 1)) if t + 1 < TILES else None)
                else:
                    qkv(layer, 0, 0, 0)
                    turn_hidden(layer, TILES - 1)
                    for t in range(1, TILES):
                        qkv(layer, 0, 0, t)
                if layer == 1:
                    logf()
                zproj(layer, 0, 0)
                if layer == 1:
                    cumulate()
                turn_qk(layer, 0)

            def period(layer, h, s):
                qkv(layer, h + 1, 1 - s, 0)
                scores(layer, h, s)
                qkv(layer, h + 1, 1 - s, 1)
                qkv(layer, h + 1, 1 - s, 2)
                turn_probs(layer, h)
                qkv(layer, h + 1, 1 - s, 3)
                values(layer, h, s)
                zproj(layer, h + 1, 1 - s)
                turn_qk(layer, h + 1)

            def last(layer):
                g = HEADS * (layer + 1)
                u = TILES * OUT_CHUNKS * layer
                h = HEADS - 1
                pe.wait_ge(wlo_set, KC * (JOBS * layer + HEADS + 1))
                pe.wait_ge(ylo_set, g - 1)
                pe.wait_ge(vlo_set, TILES * g)
                project(layer, 0, 0, range(7), True, False)
                scores(layer, h, 1)
                project(layer, 0, 1, range(7), True, False)
                project(layer, 0, 3, range(5), True, False)
                turn_probs(layer, h)
                project(layer, 0, 3, range(5, 7), False, False)
                pe.wait_ge(gate_set, g)
                project(layer, 0, 2, range(3), True, False)
                values(layer, h, 1)
                project(layer, 0, 2, range(3, 7), False, False)
                pe.wait_ge(ylo_set, g)
                for t in range(TILES):
                    project(layer, 0, t, [h], False, True)
                pe.wait_ge(wlo_set, KC * (JOBS * layer + HEADS + 2))
                for t in range(TILES):
                    pe.wait_ge(x_added, u + 1 + t)
                    if layer + 1 == LAYERS and t == TILES - 1:
                        for part in out_parts[-2:]:
                            project_part(*part)
                    else:
                        project(layer, 1, t, range(HEADS), True, True)
                    if layer + 1 < LAYERS and t >= 1:
                        turn_hidden(layer + 1, t - 1)

            for layer in range(LAYERS):
                heads_loop(pe, layer, first, period, last)

        @block.scalar
        def _(act):
            def split_w(layer, h, slot, ks):
                j = JOBS * layer + h
                for k in ks:
                    if k == 0:
                        if isinstance(h, int) and h < 2:
                            wait(act, o_done, TILES * (OUT_CHUNKS * (layer - 1) + h + 1))
                        else:
                            wait(act, z_done, HEADS * layer + h - 1)
                    raw = w_raw[:, k % RAW, :]
                    if isinstance(j, int) and j == 0:
                        raw = first_raw[:, k, :]
                        act.wait_ge(first_in[k], 16)
                    else:
                        act.wait_ge(raw_in[k % RAW], 16 * (2 * (j - 1) + k // RAW + 1))
                    act.activation(w_hi[:, slot, k, :], raw, ACT.Copy).then_inc(whi_set, 1)

            def square_x(layer, t):
                n = TILES * layer + t
                if layer == 0:
                    act.wait_ge(x_in[t], 16)
                else:
                    act.wait_ge(x_added, TILES * OUT_CHUNKS * layer - TILES + t + 1)
                act.activation(hT_hi[:, :, t * P:(t + 1) * P], xs[:, t, :].rearrange("p (k n) -> p k n", k=KC),
                               ACT.Square, scale=DM ** -0.5, accum_out=ssx[:, t, 0:1]).then_inc(xsq_set, 1)

            def split_hidden(layer, t):
                n = TILES * layer + t
                for half in range(2):
                    act.wait_ge(hT_turned, 2 * n + half + 1)
                    act.activation(hT_hi[:, 4 * half:4 * half + 4, t * P:(t + 1) * P],
                                   banks[:, QT_BANK + half, :].rearrange("p (k n) -> p k n", k=4),
                                   ACT.Copy).then_inc(hThi_set, 1)

            def read_qkv(layer, h, s, t):
                a = TILES * (HEADS * layer + h) + t
                act.wait_ge(a_done, a + 1)
                wait(act, rstd_set, a - 1)
                wait(act, ssq_set, a - 1)
                for m in range(2):
                    sq = act.activation(junk[:, 2 * (t % 2) + m, :], banks[:, t % 2, m * P:(m + 1) * P],
                                        ACT.Square, scale=SCALE, accum_out=ssq[:, t % 2, m:m + 1])
                sq.then_inc(ssq_set, 1)
                act.activation(v_hi[:, s, t, :], banks[:, t % 2, 2 * P:3 * P], ACT.Copy).then_inc(vhi_set, 1)

            def split_qk(layer, h):
                g = HEADS * layer + h
                for m in range(2):
                    act.wait_ge(qk_turned, 2 * g + m + 1)
                    act.activation(qkT_hi[:, m, :], banks[:, QT_BANK + m, :], ACT.Copy).then_inc(qkThi_set, 1)

            def exps(layer, h):
                g = HEADS * layer + h
                wait(act, p_turned, 3 * g)
                for n, t in enumerate(T_ORDER):
                    bank, col = S_AT[t]
                    w = P * (t + 1)
                    act.wait_ge(max_set, TILES * g + (n + 1 if n < 2 else TILES))
                    act.activation(probs[:, P_COL[t]:P_COL[t] + w], banks[:, bank, col:col + w], ACT.Exp,
                                   bias=negmax[:, t:t + 1], accum_out=rowsum[:, t:t + 1]).then_inc(exp_set, 1)

            def split_probs(layer, h):
                g = HEADS * layer + h
                for n, js in enumerate(PT_GROUPS):
                    w = sum(SEQ - j * P for j in js)
                    c = PT_COL[js[0]]
                    act.wait_ge(p_turned, 3 * g + n + 1)
                    act.activation(pT_hi[:, c:c + w], banks[:, PT_AT[js[0]][0], 0:w], ACT.Copy).then_inc(pThi_set, 1)

            def split_y(layer, h):
                g = HEADS * layer + h
                act.wait_ge(y_gated, g + 1)
                act.activation(yT_hi[:, bass.ds(h, 1), :].rearrange("p a n -> p (a n)"), gz[:, 1, :],
                               ACT.Copy).then_inc(yhi_set, 1)

            def exp_z(layer, h):
                g = HEADS * layer + h
                act.wait_ge(z_done, g + 1)
                wait(act, gate_set, g)
                act.activation(gz[:, 0, :], banks[:, Z_BANK, :], ACT.Exp, scale=-1.0).then_inc(ez_set, 1)

            def first(layer):
                if layer == 0:
                    square_x(layer, 0)
                    split_w(layer, 0, 0, (0, 1))
                    split_hidden(layer, 0)
                    split_w(layer, 0, 0, (2, 3))
                    square_x(layer, 1)
                    split_w(layer, 0, 0, (4, 5, 6, 7))
                    split_hidden(layer, 1)
                    square_x(layer, 2)
                    for t in range(TILES):
                        read_qkv(layer, 0, 0, t)
                        if t == 0:
                            square_x(layer, 3)
                        if t + 2 < TILES:
                            split_hidden(layer, t + 2)
                        if t + 1 < TILES:
                            split_w(layer, 1, 1, (2 * t, 2 * t + 1))
                        else:
                            act.wait_ge(small_in, 32)
                            act.activation(wf_hi[:, :, :], wf_raw[:, :, :], ACT.Copy).then_inc(wf_split, 1)
                else:
                    read_qkv(layer, 0, 0, 0)
                    split_hidden(layer, TILES - 1)
                    for t in range(1, TILES):
                        split_w(layer, 1, 1, (2 * t - 2, 2 * t - 1))
                        read_qkv(layer, 0, 0, t)
                split_w(layer, 1, 1, (6, 7))
                if layer == 1:
                    act.wait_ge(f_step, 2)
                    act.activation(flog[:, 1, :, :], flog[:, 1, :, :], ACT.Exp, scale=-1.0).then_inc(f_act, 1)
                    act.wait_ge(f_step, 3)
                    act.activation(flog[:, 2, :, :], flog[:, 1, :, :], ACT.Ln).then_inc(f_act, 1)
                exp_z(layer, 0)
                if layer == 1:
                    act.wait_ge(cum_done, 1)
                    act.wait_ge(consts_set, 1)
                    act.activation(crows[0:HEADS, :], banks[0:HEADS, CUM_BANK, :], ACT.Copy,
                                   scale=-1.0).then_inc(chi_set, 1)
                split_qk(layer, 0)

            def period(layer, h, s):
                read_qkv(layer, h + 1, 1 - s, 0)
                split_w(layer, h + 2, s, (0, 1, 2, 3))
                exps(layer, h)
                read_qkv(layer, h + 1, 1 - s, 1)
                split_w(layer, h + 2, s, (4,))
                read_qkv(layer, h + 1, 1 - s, 2)
                split_probs(layer, h)
                split_w(layer, h + 2, s, (5, 6, 7))
                read_qkv(layer, h + 1, 1 - s, 3)
                split_y(layer, h)
                split_qk(layer, h + 1)
                exp_z(layer, h + 1)

            def last(layer):
                h = HEADS - 1
                exps(layer, h)
                split_w(layer, h + 2, 1, (0, 1, 2, 3, 4))
                split_probs(layer, h)
                split_w(layer, h + 2, 1, (5, 6, 7))
                split_y(layer, h)
                if layer + 1 < LAYERS:
                    for t in range(TILES):
                        split_w(layer + 1, 0, 0, (2 * t, 2 * t + 1))
                        square_x(layer + 1, t)
                        if t >= 1:
                            split_hidden(layer + 1, t - 1)

            for layer in range(LAYERS):
                heads_loop(act, layer, first, period, last)

        @block.vector
        def _(dve):
            def norm_x(layer, t):
                n = TILES * layer + t
                buf = normed(layer, t)
                dve.wait_ge(xrs_set, n + 1)
                dve.wait_ge(gain_in[layer], 16)
                wait(dve, hT_turned, 2 * (n - 1) if layer or t == 3 else 0)
                for half in range(2):
                    cols = slice(half * DM // 2, (half + 1) * DM // 2)
                    dve.scalar_tensor_tensor(out=buf[:, cols], in0=xs[:, t, cols], scalar=ssx[:, t, 1:2],
                                             in1=gz[:, half, :], op0=ALU.mult, op1=ALU.mult).then_inc(xn_set, 1)

            def split_hidden(layer, t):
                n = TILES * layer + t
                for half in range(2):
                    dve.wait_ge(hThi_set, 2 * n + half + 1)
                    dst = slice(4 * half, 4 * half + 4), slice(t * P, (t + 1) * P)
                    dve.tensor_tensor(hT_lo[:, dst[0], dst[1]],
                                      banks[:, QT_BANK + half, :].rearrange("p (k n) -> p k n", k=4),
                                      f32(hT_hi[:, dst[0], dst[1]]), ALU.subtract).then_inc(hTlo_set, 1)

            def split_w_odd(ks):
                for k in ks:
                    dve.wait_ge(whi_set, k + 1)
                    dve.tensor_tensor(w_lo[:, 0, k, :], first_raw[:, k, :], f32(w_hi[:, 0, k, :]),
                                      ALU.subtract).then_inc(wlo_odd, 1)

            def rope_tables():
                dve.wait_ge(tables_in, 64)
                dve.tensor_scalar(gains[:, 0, :], gains[:, 0, :], SCALE, None, ALU.mult).then_inc(tables_set, 1)
                dve.wait_ge(tables_set, 1)
                half = P // 2
                for m in range(2):
                    for a in range(2):
                        last = dve.tensor_tensor(sin_t[:, :, m, a * half:(a + 1) * half],
                                                 sin_t[:, :, 1, a * half:(a + 1) * half],
                                                 bcast(gains[:, m, (1 - a) * half:(2 - a) * half], TILES), ALU.mult)
                last.then_inc(tables_set, 1)

            def rot_steps(layer, h, t):
                return 3 * (TILES * h + t) if layer == 0 else 3 * TILES * HEADS + TILES * h + t

            def read_qkv(layer, h, s, t):
                a = TILES * (HEADS * layer + h) + t
                qk = banks[:, t % 2, 0:2 * P].rearrange("p (m n) -> p m n", m=2)
                r = rot_steps(layer, h, t)
                dve.wait_ge(vhi_set, a + 1)
                wait(dve, qkn_set, a)
                if layer == 0:
                    dve.tensor_tensor(rot[:, 0], qk, cos_t[:, t], ALU.mult).then_inc(rot_set, 1)
                    swapped = banks[:, t % 2, 0:2 * P].rearrange("p (m a n) -> p m a n", m=2, a=2)[:, :, ::-1, :]
                    dve.tensor_tensor(rot[:, 1].rearrange("p m (a n) -> p m a n", a=2), swapped,
                                      sin_t[:, t].rearrange("p m (a n) -> p m a n", a=2), ALU.mult).then_inc(rot_set, 1)
                else:
                    dve.tensor_tensor(rot[:, 0], qk, cos_t[:, 0], ALU.mult).then_inc(rot_set, 1)
                dve.tensor_tensor(v_lo[:, s, t, :], banks[:, t % 2, 2 * P:3 * P], f32(v_hi[:, s, t, :]),
                                  ALU.subtract).then_inc(vlo_set, 1)
                if layer == 0:
                    dve.wait_ge(rot_set, r + 2)
                    dve.tensor_tensor(rot[:, 0], rot[:, 0], rot[:, 1], ALU.add).then_inc(rot_set, 1)

            def norm_qk(layer, h, t):
                a = TILES * (HEADS * layer + h) + t
                dve.wait_ge(rot_set, rot_steps(layer, h, t) + (3 if layer == 0 else 1))
                dve.wait_ge(rstd_set, a + 1)
                for m in range(2):
                    last = dve.tensor_scalar(qkn[:, t, m, :], rot[:, 0, m, :], rstd[:, t % 2, m:m + 1], None, ALU.mult)
                last.then_inc(qkn_set, 1)

            def split_qk(layer, h):
                g = HEADS * layer + h
                for m in range(2):
                    dve.wait_ge(qkThi_set, 2 * g + m + 1)
                    dve.tensor_tensor(qkT_lo[:, m, :], banks[:, QT_BANK + m, :], f32(qkT_hi[:, m, :]),
                                      ALU.subtract).then_inc(qkTlo_set, 1)

            def maxima(layer, h):
                g = HEADS * layer + h

                def mask_tile(n):
                    t = T_ORDER[n]
                    bank, col = S_AT[t]
                    block_at = banks[:, bank, col + P * t:col + P * (t + 1)]
                    dve.wait_ge(s_done, 3 * g + min(n, 2) + 1)
                    dve.tensor_tensor(block_at, block_at, mask[:, :], ALU.add).then_inc(mask_added, 1)

                wait(dve, exp_set, TILES * g)
                mask_tile(0)
                for n, t in enumerate(T_ORDER):
                    bank, col = S_AT[t]
                    if n + 1 < TILES:
                        mask_tile(n + 1)
                    dve.wait_ge(mask_added, TILES * g + n + 1)
                    dve.tensor_reduce(negmax[:, t:t + 1], banks[:, bank, col:col + P * (t + 1)], AX.X, ALU.max,
                                      negate=True).then_inc(max_set, 1)

            def normalise(layer, h):
                g = HEADS * layer + h
                for n, t in enumerate(T_ORDER):
                    dve.wait_ge(exp_set, TILES * g + n + 1)
                    dve.reciprocal(rinv[:, t:t + 1], rowsum[:, t:t + 1]).then_inc(rinv_set, 1)
                for n, t in enumerate(T_ORDER):
                    p = probs[:, P_COL[t]:P_COL[t] + P * (t + 1)]
                    dve.wait_ge(rinv_set, TILES * g + n + 1)
                    dve.tensor_scalar(p, p, rinv[:, t:t + 1], None, ALU.mult).then_inc(probs_set, 1)

            def split_probs(layer, h):
                g = HEADS * layer + h
                for n, js in enumerate(PT_GROUPS):
                    w = sum(SEQ - j * P for j in js)
                    c = PT_COL[js[0]]
                    dve.wait_ge(pThi_set, 3 * g + n + 1)
                    dve.tensor_tensor(pT_lo[:, c:c + w], banks[:, PT_AT[js[0]][0], 0:w], f32(pT_hi[:, c:c + w]),
                                      ALU.subtract).then_inc(pTlo_set, 1)

            def gate_y(layer, h):
                g = HEADS * layer + h
                dve.wait_ge(y_done, g + 1)
                dve.wait_ge(gate_set, g + 1)
                dve.tensor_tensor(gz[:, 1, :], banks[:, Y_BANK, :], gz[:, 1, :], ALU.mult).then_inc(y_gated, 1)
                dve.wait_ge(yhi_set, g + 1)
                row = bass.ds(h, 1)
                dve.tensor_tensor(yT_lo[:, row, :].rearrange("p a n -> p (a n)"), gz[:, 1, :],
                                  f32(yT_hi[:, row, :].rearrange("p a n -> p (a n)")),
                                  ALU.subtract).then_inc(ylo_set, 1)

            def silu(layer, h):
                g = HEADS * layer + h
                dve.wait_ge(ez_set, g + 1)
                dve.tensor_scalar(gz[:, 0, :], gz[:, 0, :], 1.0, None, ALU.add).then_inc(ez1_set, 1)

            def silu_part(layer, h, n):
                g = HEADS * layer + h
                part = gz[:, 0, n * P:(n + 1) * P]
                if n == 0:
                    dve.wait_ge(ez1_set, 5 * g + 1)
                dve.reciprocal(part, part).then_inc(ez1_set, 1)
                if n == 3:
                    dve.wait_ge(ez1_set, 5 * g + 5)
                    wait(dve, ylo_set, g)
                    dve.tensor_tensor(gz[:, 1, :], banks[:, Z_BANK, :], gz[:, 0, :], ALU.mult).then_inc(gate_set, 1)

            def set_pick(h, s):
                wait(dve, s_done, 3 * (HEADS + h - 1))
                dve.tensor_scalar(pick[:, s, :], ident[:, :], 0.0, onehot[:, bass.ds(h, 1)],
                                  ALU.mult, ALU.add).then_inc(pick_set, 1)

            def add_unit(layer, u):
                c, t = divmod(u, TILES)
                n = TILES * OUT_CHUNKS * layer + u
                dve.wait_ge(o_done, n + 1)
                part = xs[:, t, c * CH:(c + 1) * CH]
                dve.tensor_tensor(part, banks[:, unit_bank(c, t), :], part, ALU.add).then_inc(x_added, 1)

            def add_part(n, bank, t, cols):
                dve.wait_ge(o_done, TILES * OUT_CHUNKS * (LAYERS - 1) + n + 1)
                dve.tensor_tensor(xs[:, t, cols], banks[:, bank, 0:cols.stop - cols.start], xs[:, t, cols],
                                  ALU.add).then_inc(x_added, 1)

            def log_sigmoid():
                f, e, ln, lf = (flog[:, n] for n in range(4))
                dve.wait_ge(f_done, 1)
                dve.tensor_tensor(f, banks[:, LOGF_BANK, 0:TILES * HEADS].rearrange("p (t h) -> p t h", t=TILES),
                                  bcast(fbias[:, :], TILES), ALU.add).then_inc(f_step, 1)
                dve.wait_ge(f_step, 1)
                dve.scalar_tensor_tensor(out=e, in0=f, scalar=-1.0, in1=f, op0=ALU.mult,
                                         op1=ALU.max).then_inc(f_step, 1)
                dve.wait_ge(f_act, 1)
                dve.tensor_scalar(e, e, 1.0, None, ALU.add).then_inc(f_step, 1)
                dve.wait_ge(f_act, 2)
                dve.scalar_tensor_tensor(out=lf, in0=f, scalar=0.0, in1=ln, op0=ALU.min,
                                         op1=ALU.subtract).then_inc(f_step, 1)

            def first(layer):
                if layer == 0:
                    norm_x(layer, 0)
                    split_w_odd((1,))
                    split_hidden(layer, 0)
                    split_w_odd((3,))
                    norm_x(layer, 1)
                    split_w_odd((5, 7))
                    split_hidden(layer, 1)
                    norm_x(layer, 2)
                    rope_tables()
                    split_hidden(layer, 2)
                    dve.wait_ge(tables_set, 3)
                    read_qkv(layer, 0, 0, 0)
                    norm_x(layer, 3)
                    norm_qk(layer, 0, 0)
                    read_qkv(layer, 0, 0, 1)
                    norm_qk(layer, 0, 1)
                    split_hidden(layer, 3)
                    for t in range(2, TILES):
                        read_qkv(layer, 0, 0, t)
                        norm_qk(layer, 0, t)
                    dve.wait_ge(wf_split, 1)
                    dve.tensor_tensor(wf_lo[:, :, :], wf_raw[:, :, :], f32(wf_hi[:, :, :]),
                                      ALU.subtract).then_inc(wf_split, 1)
                else:
                    dve.wait_ge(qk_gain_in, 32)
                    dve.tensor_scalar(cos_t[:, 0, 0, :], cos_t[:, 0, 0, :], SCALE, None, ALU.mult).then_inc(tables_set, 1)
                    dve.wait_ge(tables_set, 4)
                    read_qkv(layer, 0, 0, 0)
                    norm_qk(layer, 0, 0)
                    split_hidden(layer, TILES - 1)
                    for t in range(1, TILES):
                        read_qkv(layer, 0, 0, t)
                        norm_qk(layer, 0, t)
                    log_sigmoid()
                    dve.wait_ge(consts_set, 1)
                    set_pick(0, 0)
                if layer == 1:
                    dve.wait_ge(chi_set, 1)
                    dve.scalar_tensor_tensor(out=crows[32:32 + HEADS, :], in0=banks[0:HEADS, CUM_BANK, :], scalar=-1.0,
                                             in1=f32(crows[0:HEADS, :]), op0=ALU.mult,
                                             op1=ALU.subtract).then_inc(c_set, 1)
                split_qk(layer, 0)

            def period(layer, h, s):
                read_qkv(layer, h + 1, 1 - s, 0)
                silu(layer, h)
                norm_qk(layer, h + 1, 0)
                maxima(layer, h)
                silu_part(layer, h, 0)
                normalise(layer, h)
                read_qkv(layer, h + 1, 1 - s, 1)
                silu_part(layer, h, 1)
                norm_qk(layer, h + 1, 1)
                silu_part(layer, h, 2)
                split_probs(layer, h)
                silu_part(layer, h, 3)
                read_qkv(layer, h + 1, 1 - s, 2)
                norm_qk(layer, h + 1, 2)
                read_qkv(layer, h + 1, 1 - s, 3)
                gate_y(layer, h)
                norm_qk(layer, h + 1, 3)
                if layer == 1:
                    set_pick(h + 1, 1 - s)
                split_qk(layer, h + 1)

            def last(layer):
                h = HEADS - 1
                silu(layer, h)
                maxima(layer, h)
                silu_part(layer, h, 0)
                normalise(layer, h)
                for n in range(1, 4):
                    silu_part(layer, h, n)
                split_probs(layer, h)
                gate_y(layer, h)
                if layer + 1 == LAYERS:
                    for n, part in enumerate(out_parts):
                        add_part(n, *part)
                    return
                for u in range(TILES * OUT_CHUNKS):
                    add_unit(layer, u)
                    t = u - TILES
                    if t >= 0:
                        norm_x(layer + 1, t)
                        if t >= 1:
                            split_hidden(layer + 1, t - 1)

            for layer in range(LAYERS):
                heads_loop(dve, layer, first, period, last)

        @block.gpsimd
        def _(pool):
            def split_w(layer, h, slot, ks, by=1):
                j = JOBS * layer + h
                for k in ks:
                    wait(pool, whi_set, KC * j + k + 1)
                    raw = first_raw[:, k, :] if isinstance(j, int) and j == 0 else w_raw[:, k % RAW, :]
                    pool.tensor_tensor(w_lo[:, slot, k, :], raw, f32(w_hi[:, slot, k, :]),
                                       ALU.subtract).then_inc(wlo_set, by)

            def rstd_x(layer, t):
                n = TILES * layer + t
                pool.wait_ge(xsq_set, n + 1)
                pool.tensor_tensor(msx[:, t:t + 1], ssx[:, t, 0:1], eps[:, 0:1], ALU.add).then_inc(xms_set, 1)
                pool.wait_ge(xms_set, n + 1)
                pool.tensor_tensor(ssx[:, t, 1:2], msx[:, t:t + 1], power[:, 0:1],
                                   ALU.pow).then_inc(xrs_set, 1)

            def rstd_qk(layer, h, t):
                a = TILES * (HEADS * layer + h) + t
                pool.wait_ge(ssq_set, a + 1)
                wait(pool, qkn_set, a - 1)
                pool.tensor_tensor(msq[:, t % 2, :], ssq[:, t % 2, :], eps[:, :], ALU.add).then_inc(msq_set, 1)
                pool.wait_ge(msq_set, a + 1)
                pool.tensor_tensor(rstd[:, t % 2, :], msq[:, t % 2, :], power[:, :], ALU.pow).then_inc(rstd_set, 1)

            pool.memset(ident[:, :], 0.0)
            pool.memset(mask[:, :], 0.0)
            pool.memset(onehot[:, :], 0.0)
            pool.memset(f32(crows[:, :]), 0.0)
            pool.memset(eps[:, :], EPS)
            pool.memset(power[:, :], -0.5).then_inc(const_steps, 1)
            pool.wait_ge(const_steps, 1)
            pool.affine_select(out=ident[:, :], in_=ident[:, :], compare_op=ALU.not_equal, fill=1.0, base=0,
                               pattern=[[-1, P]], channel_multiplier=1)
            pool.affine_select(out=mask[:, :], in_=mask[:, :], compare_op=ALU.is_ge, fill=MASKED, base=0,
                               pattern=[[-1, P]], channel_multiplier=1)
            pool.affine_select(out=onehot[:, :], in_=onehot[:, :], compare_op=ALU.not_equal, fill=1.0, base=0,
                               pattern=[[-1, HEADS]], channel_multiplier=1).then_inc(const_steps, 1)
            pool.wait_ge(const_steps, 2)
            pool.affine_select(out=onehot[:, :], in_=onehot[:, :], compare_op=ALU.not_equal, fill=1.0, base=-32,
                               pattern=[[-1, HEADS]], channel_multiplier=1).then_inc(consts_set, 1)
            pool.wait_ge(consts_set, 1)

            def first(layer):
                if layer == 0:
                    rstd_x(layer, 0)
                    split_w(layer, 0, 0, (0, 2), by=2)
                    rstd_x(layer, 1)
                    split_w(layer, 0, 0, (4, 6), by=2)
                    rstd_x(layer, 2)
                    pool.wait_ge(tables_set, 1)
                    for m in range(2):
                        folded = pool.tensor_tensor(cos_t[:, :, m, :], cos_t[:, :, 1, :],
                                                    bcast(gains[:, m, :], TILES), ALU.mult)
                    folded.then_inc(tables_set, 1)
                    rstd_x(layer, 3)
                else:
                    tri = sin_t[:, :, :, :].rearrange("p a b n -> p (a b n)")[:, 0:SEQ]
                    pool.wait_ge(qkn_set, TILES * HEADS)
                    pool.memset(tri, 1.0).then_inc(tri_set, 1)
                    pool.wait_ge(tri_set, 1)
                    pool.affine_select(out=tri, in_=tri, compare_op=ALU.is_ge, fill=0.0, base=0,
                                       pattern=[[1, SEQ]], channel_multiplier=-1).then_inc(tri_set, 1)
                rstd_qk(layer, 0, 0)
                for t in range(1, TILES):
                    split_w(layer, 1, 1, (2 * t - 2, 2 * t - 1))
                    rstd_qk(layer, 0, t)
                split_w(layer, 1, 1, (6, 7))

            def period(layer, h, s):
                rstd_qk(layer, h + 1, 0)
                split_w(layer, h + 2, s, (0, 1, 2, 3))
                rstd_qk(layer, h + 1, 1)
                split_w(layer, h + 2, s, (4,))
                rstd_qk(layer, h + 1, 2)
                split_w(layer, h + 2, s, (5, 6, 7))
                rstd_qk(layer, h + 1, 3)

            def last(layer):
                split_w(layer, HEADS + 1, 1, range(KC))
                if layer + 1 < LAYERS:
                    for t in range(TILES):
                        split_w(layer + 1, 0, 0, (2 * t, 2 * t + 1))
                        rstd_x(layer + 1, t)

            for layer in range(LAYERS):
                heads_loop(pool, layer, first, period, last)


_INS = ["x", "norm_g", "w_out", "a_w_in", "a_q_norm", "a_k_norm", "b_w_in", "b_f_bias", "b_q_norm", "b_k_norm"]
_OUT = ((1, SEQ, DM), "float32")


def rope_constants():
    import numpy as np

    half = P // 2
    inv = 1.0 / np.float32(10000.0) ** (np.arange(0, P, 2, dtype=np.float32) / np.float32(P))
    ang = np.arange(SEQ, dtype=np.float32)[:, None] * inv.astype(np.float32)[None, :]
    cos, sin = np.cos(ang).astype(np.float32), np.sin(ang).astype(np.float32)
    assert cos.shape == (SEQ, half)
    return np.concatenate([cos, cos], 1), np.concatenate([-sin, sin], 1)


def kernel(**inputs):
    import numpy as np
    import concourse.bacc as bacc
    from concourse.bass_utils import run_bass_kernel_spmd

    nc = bacc.Bacc("TRN2", target_bir_lowering=False, num_devices=1)
    given = {name: np.ascontiguousarray(inputs[name]) for name in _INS}
    given["rope_cos"], given["rope_sin"] = rope_constants()
    arrays, args = {}, []
    for name, a in given.items():
        arrays[f"in_{name}_dram"] = a
        args.append(nc.dram_tensor(f"in_{name}_dram", a.shape, mybir.dt.from_np(a.dtype), kind="ExternalInput").ap())
    shape, dtype = _OUT
    args.append(nc.dram_tensor("out_0_dram", shape, mybir.dt.from_np(np.dtype(dtype)), kind="ExternalOutput").ap())
    build_trunk(nc, *args)
    r = run_bass_kernel_spmd(nc, [arrays], core_ids=[0])
    return r.results[0]["out_0_dram"]
```
